# Optimizing a Trainium2 kernel written in Bass

```python
import jax, jax.numpy as jnp
from jax import lax
import numpy as np

D_MODEL = 2048
BATCH = 1
SEQ = 256
DEPTH = 1

HEAD_DIM = 128
N_ATTN_HEADS = 8
ATTN_WIDTH = N_ATTN_HEADS * HEAD_DIM
CONV_WIDTH = D_MODEL - ATTN_WIDTH
CONV_GROUPS = CONV_WIDTH // HEAD_DIM
CONV_KSIZE = 3
IN_PROJ_WIDTH = 3 * ATTN_WIDTH + 3 * CONV_WIDTH

MOBA_BLOCK = 256
MOBA_TOPK = 3
QUERY_CHUNK = 32
ROPE_THETA = 10000.0

N_MEM = 256
N_XATTN_HEADS = 4
XATTN_HEAD_DIM = 128
XATTN_WIDTH = N_XATTN_HEADS * XATTN_HEAD_DIM

D_FF = -(-(8 * D_MODEL) // (3 * 256)) * 256
EPS = 1e-6

kernel_name = "hymba_moba_shortconv_hybrid_layer"

def rms_norm(x, g):
    xf = x.astype(jnp.float32)
    y = xf * lax.rsqrt(jnp.mean(xf * xf, axis=-1, keepdims=True) + EPS)
    return (y * g.astype(jnp.float32)).astype(x.dtype)

def rope_tables(positions):
    inv_freq = ROPE_THETA ** (-jnp.arange(0, HEAD_DIM, 2, dtype=jnp.float32) / HEAD_DIM)
    ang = positions.astype(jnp.float32)[..., None] * inv_freq
    return jnp.cos(ang), jnp.sin(ang)

def apply_rope(t, cos, sin):
    t1, t2 = jnp.split(t.astype(jnp.float32), 2, axis=-1)
    c = cos[:, :, None, :]
    s = sin[:, :, None, :]
    return jnp.concatenate([t1 * c - t2 * s, t2 * c + t1 * s], axis=-1).astype(t.dtype)

def moba_attention(q, k, v):
    bsz, n_h, s_len, hd = q.shape
    n_blk = -(-s_len // MOBA_BLOCK)
    s_pad = n_blk * MOBA_BLOCK
    top_k = min(MOBA_TOPK, n_blk)
    pad = ((0, 0), (0, 0), (0, s_pad - s_len), (0, 0))
    kp = jnp.pad(k, pad)
    vp = jnp.pad(v, pad)
    kb = kp.reshape(bsz, n_h, n_blk, MOBA_BLOCK, hd)
    vb = vp.reshape(bsz, n_h, n_blk, MOBA_BLOCK, hd)
    k_mean = jnp.mean(kb.astype(jnp.float32), axis=3)
    scale = hd ** -0.5
    b_idx = jnp.arange(bsz)[:, None, None, None]
    h_idx = jnp.arange(n_h)[None, :, None, None]
    blk_ids = jnp.arange(n_blk)
    key_off = jnp.arange(MOBA_BLOCK)

    def one_chunk(c):
        q0 = c * QUERY_CHUNK
        qc = lax.dynamic_slice_in_dim(q, q0, QUERY_CHUNK, axis=2)
        blk = q0 // MOBA_BLOCK
        qpos = q0 + jnp.arange(QUERY_CHUNK)
        gate = jnp.einsum('bhqd,bhnd->bhqn', qc.astype(jnp.float32), k_mean)
        gate = jnp.where(blk_ids < blk, gate, -jnp.inf)
        top_val, top_idx = lax.top_k(gate, top_k)
        sel_valid = jnp.isfinite(top_val)
        k_sel = kb[b_idx, h_idx, top_idx]
        v_sel = vb[b_idx, h_idx, top_idx]
        s_sel = jnp.einsum('bhqd,bhqrkd->bhqrk', qc, k_sel).astype(jnp.float32) * scale
        s_sel = jnp.where(sel_valid[..., None], s_sel, -jnp.inf)
        k_own = lax.dynamic_slice_in_dim(kp, blk * MOBA_BLOCK, MOBA_BLOCK, axis=2)
        v_own = lax.dynamic_slice_in_dim(vp, blk * MOBA_BLOCK, MOBA_BLOCK, axis=2)
        s_own = jnp.einsum('bhqd,bhkd->bhqk', qc, k_own).astype(jnp.float32) * scale
        kpos = blk * MOBA_BLOCK + key_off
        s_own = jnp.where(kpos[None, :] <= qpos[:, None], s_own, -jnp.inf)
        s_all = jnp.concatenate(
            [s_sel.reshape(bsz, n_h, QUERY_CHUNK, top_k * MOBA_BLOCK), s_own], axis=-1)
        p = jax.nn.softmax(s_all, axis=-1)
        p_sel = p[..., :top_k * MOBA_BLOCK].reshape(
            bsz, n_h, QUERY_CHUNK, top_k, MOBA_BLOCK).astype(v.dtype)
        p_own = p[..., top_k * MOBA_BLOCK:].astype(v.dtype)
        return (jnp.einsum('bhqrk,bhqrkd->bhqd', p_sel, v_sel)
                + jnp.einsum('bhqk,bhkd->bhqd', p_own, v_own))

    out = lax.map(one_chunk, jnp.arange(s_len // QUERY_CHUNK))
    return out.transpose(1, 2, 0, 3, 4).reshape(bsz, n_h, s_len, hd)

def short_conv(u, w_conv, b_conv):
    kern = w_conv[:, None, :].astype(u.dtype)
    y = lax.conv_general_dilated(
        u, kern, window_strides=(1,), padding=[(CONV_KSIZE - 1, 0)],
        dimension_numbers=('NWC', 'WIO', 'NWC'), feature_group_count=u.shape[-1])
    return y + b_conv

def hybrid_mixer(h, cos, sin, w_in, w_conv, b_conv, g_attn_out, g_conv_out, w_out):
    bsz, s_len, _ = h.shape
    proj = h @ w_in
    q, k, v, c_gate, b_gate, x_in = jnp.split(
        proj, np.cumsum([ATTN_WIDTH] * 3 + [CONV_WIDTH] * 2).tolist(), axis=-1)
    q = apply_rope(q.reshape(bsz, s_len, N_ATTN_HEADS, HEAD_DIM), cos, sin)
    k = apply_rope(k.reshape(bsz, s_len, N_ATTN_HEADS, HEAD_DIM), cos, sin)
    v = v.reshape(bsz, s_len, N_ATTN_HEADS, HEAD_DIM)
    o_attn = moba_attention(q.transpose(0, 2, 1, 3), k.transpose(0, 2, 1, 3),
                            v.transpose(0, 2, 1, 3)).transpose(0, 2, 1, 3)
    o_attn = rms_norm(o_attn, g_attn_out.reshape(N_ATTN_HEADS, HEAD_DIM))
    y_conv = b_gate * short_conv(c_gate * x_in, w_conv, b_conv)
    y_conv = rms_norm(y_conv.reshape(bsz, s_len, CONV_GROUPS, HEAD_DIM),
                      g_conv_out.reshape(CONV_GROUPS, HEAD_DIM))
    merged = jnp.concatenate([o_attn.reshape(bsz, s_len, ATTN_WIDTH),
                              y_conv.reshape(bsz, s_len, CONV_WIDTH)], axis=-1)
    return merged @ w_out

def memory_cross_attention(h, m, w_xq, w_xkv, w_xo):
    bsz, s_len, _ = h.shape
    q = (h @ w_xq).reshape(bsz, s_len, N_XATTN_HEADS, XATTN_HEAD_DIM)
    kv = (m @ w_xkv).reshape(bsz, m.shape[1], 2, N_XATTN_HEADS, XATTN_HEAD_DIM)
    k, v = kv[:, :, 0], kv[:, :, 1]
    s = jnp.einsum('bqhd,bmhd->bhqm', q, k).astype(jnp.float32) * (XATTN_HEAD_DIM ** -0.5)
    p = jax.nn.softmax(s, axis=-1).astype(v.dtype)
    o = jnp.einsum('bhqm,bmhd->bqhd', p, v).reshape(bsz, s_len, XATTN_WIDTH)
    return o @ w_xo

def swiglu(h, w_gate, w_up, w_down):
    return (jax.nn.silu(h @ w_gate) * (h @ w_up)) @ w_down

def setup_inputs(seed: int = 0) -> dict:
    key = jax.random.key(seed)
    ks = jax.random.split(key, 24)
    f32 = jnp.float32

    def nrm(k, shape, fan_in):
        return jax.random.normal(k, shape, f32) * (fan_in ** -0.5)

    def gain(k, shape):
        return 1.0 + 0.02 * jax.random.normal(k, shape, f32)

    x = jax.random.normal(ks[0], (BATCH, SEQ, D_MODEL), f32)
    mem = jax.random.normal(ks[1], (BATCH, N_MEM, D_MODEL), f32)
    offset = jax.random.randint(ks[2], (BATCH, 1), 0, SEQ, dtype=jnp.int32)
    positions = (offset + jnp.arange(SEQ, dtype=jnp.int32)[None, :]).astype(jnp.int32)
    return {
        "x": x,
        "mem": mem,
        "positions": positions,
        "g_mix": gain(ks[3], (DEPTH, D_MODEL)),
        "w_in": nrm(ks[4], (DEPTH, D_MODEL, IN_PROJ_WIDTH), D_MODEL),
        "w_conv": nrm(ks[5], (DEPTH, CONV_KSIZE, CONV_WIDTH), CONV_KSIZE),
        "b_conv": 0.02 * jax.random.normal(ks[6], (DEPTH, CONV_WIDTH), f32),
        "g_attn_out": gain(ks[7], (DEPTH, ATTN_WIDTH)),
        "g_conv_out": gain(ks[8], (DEPTH, CONV_WIDTH)),
        "w_out": nrm(ks[9], (DEPTH, D_MODEL, D_MODEL), D_MODEL),
        "g_xattn": gain(ks[10], (DEPTH, D_MODEL)),
        "g_mem": gain(ks[11], (DEPTH, D_MODEL)),
        "w_xq": nrm(ks[12], (DEPTH, D_MODEL, XATTN_WIDTH), D_MODEL),
        "w_xkv": nrm(ks[13], (DEPTH, D_MODEL, 2 * XATTN_WIDTH), D_MODEL),
        "w_xo": nrm(ks[14], (DEPTH, XATTN_WIDTH, D_MODEL), XATTN_WIDTH),
        "g_ffn": gain(ks[15], (DEPTH, D_MODEL)),
        "w_gate": nrm(ks[16], (DEPTH, D_MODEL, D_FF), D_MODEL),
        "w_up": nrm(ks[17], (DEPTH, D_MODEL, D_FF), D_MODEL),
        "w_down": nrm(ks[18], (DEPTH, D_FF, D_MODEL), D_FF),
        "g_final": gain(ks[19], (D_MODEL,)),
    }

def reference(x, mem, positions, g_mix, w_in, w_conv, b_conv, g_attn_out, g_conv_out, w_out,
              g_xattn, g_mem, w_xq, w_xkv, w_xo, g_ffn, w_gate, w_up, w_down, g_final):
    cos, sin = rope_tables(positions)
    for l in range(DEPTH):
        h = rms_norm(x, g_mix[l])
        x = x + hybrid_mixer(h, cos, sin, w_in[l], w_conv[l], b_conv[l],
                             g_attn_out[l], g_conv_out[l], w_out[l])
        h = rms_norm(x, g_xattn[l])
        m = rms_norm(mem, g_mem[l])
        x = x + memory_cross_attention(h, m, w_xq[l], w_xkv[l], w_xo[l])
        h = rms_norm(x, g_ffn[l])
        x = x + swiglu(h, w_gate[l], w_up[l], w_down[l])
    return rms_norm(x, g_final)


_drawn_inputs = setup_inputs


def setup_inputs(seed=0):
    import zlib

    import numpy as np

    out = dict(_drawn_inputs(seed))
    spreads = {}
    factors = {'b_conv': 4.653,
     'g_attn_out': 5.348,
     'g_conv_out': 5.672,
     'g_xattn': 8.0,
     'g_mem': 8.0,
     'g_ffn': 4.932,
     'g_final': 2.91}
    for name, (base, spread) in spreads.items():
        noise = np.random.default_rng([zlib.crc32(name.encode()), seed]).standard_normal(out[name].shape)
        drawn = base * np.exp(spread * noise) if base else spread * noise
        out[name] = __import__('jax').numpy.asarray(drawn.astype(out[name].dtype))
    for name, factor in factors.items():
        out[name] = (out[name] * factor).astype(out[name].dtype)
    return out
```

```python
from contextlib import ExitStack

import numpy as np
import concourse.bass as bass
from concourse import mybir

D = 2048
SEQ = 256
P = 128
TT = SEQ // P
NH = 8
HD = 128
AW = NH * HD
CW = D - AW
CB = CW // HD
NXH = 4
XW = NXH * HD
FF = -(-(8 * D) // (3 * 256)) * 256
EPS = 1e-6
SCALE = HD ** -0.5
GC = 512
KS = 2
KD = D // P
SPG = KD // KS
RING = 4
LEAD = 2

G_KV = 0
G_V = G_KV + 2 * XW // GC
G_QK = G_V + AW // GC
G_C = G_QK + 2 * AW // GC
G_X = G_C + 2 * CW // GC
G_OUT = G_X + CW // GC
G_XQ = G_OUT + D // GC
G_XO = G_XQ + XW // GC
G_FF = G_XO + D // GC
NFC = FF // GC
G_DN = G_FF + 2 * NFC
J_XO = G_XO * SPG
SXO = XW // (KS * P)
J_FF = J_XO + SXO * (D // GC)
J_DN = J_FF + 2 * NFC * SPG
SDN = FF // (KS * P)
STEPS = J_DN + SDN * (D // GC)

C_MIX, C_XATTN, C_MEM, C_FFN = 0, KD, 2 * KD, 3 * KD
C_ATTN = 4 * KD
C_CONV = C_ATTN + NH
C_WC = C_CONV + CB
C_BC = C_WC + 3 * CB
NPAR = C_BC + CB

U_MEM, U_X, U_H2, U_H3, U_FF = 0, SPG, 2 * SPG, 3 * SPG, 4 * SPG
CONV_BANKS = (6, 7, 4, 5)
MASKED = -3.0e38
ROUND = 1.5 * 2.0 ** 23
SPLIT = 2.0 ** 11


def two_pi_parts():
    parts, rest = [], 2.0 * np.pi
    for _ in range(4):
        unit = 2.0 ** (np.floor(np.log2(abs(rest))) - 11)
        parts.append(float(np.round(rest / unit) * unit))
        rest -= parts[-1]
    return parts


def build(nc, stream, x, mem, params, pos, inv_freq, g_final, out):
    f32, f32r, i32 = mybir.dt.float32, mybir.dt.float32r, mybir.dt.int32
    ALU, ACT, AX = mybir.AluOpType, mybir.ActivationFunctionType, mybir.AxisListType
    ds = bass.ds
    ctx = ExitStack()
    with ctx:
        top = nc.sbuf_base if isinstance(nc.sbuf_base, int) else nc.sbuf_base()
        place = [-(-top // 64) * 64]

        def sb(name, shape, dt=f32, at=None):
            size = 4 * int(np.prod(shape[1:]))
            where = place[0] if at is None else at[0]
            if at is None:
                place[0] += -(-size // 64) * 64
            else:
                at[0] += -(-size // 64) * 64
            return nc.alloc_sbuf_tensor_at(name, shape, dt, offset=where)

        def sem(name):
            return ctx.enter_context(nc.semaphore(name))

        res = sb("res", [P, TT, D])
        raw = sb("raw", [P, RING, KS * GC])
        whi = sb("whi", [P, RING, KS * GC], f32r)
        wlo = sb("wlo", [P, RING, KS * GC], f32r)
        yout = sb("yout", [P, TT, D], at=[place[0]])
        ahi = sb("ahi", [P, KD, SEQ], f32r)
        alo = sb("alo", [P, KD, SEQ], f32r)
        ident = sb("ident", [P, P])
        ones = sb("ones", [P, P])
        par = sb("par", [P, NPAR])
        eps = sb("eps", [P, 1])
        mhalf = sb("mhalf", [P, TT])
        ssq = sb("ssq", [P, 4, TT])
        rstd = sb("rstd", [P, 4, TT])
        vpe = sb("vpe", [P, 4, TT])
        part = sb("part", [P, TT, D // GC])
        fss = sb("fss", [P, TT])
        fvar = sb("fvar", [P, TT])
        frstd = sb("frstd", [P, TT])
        shared = place[0]
        bhi = sb("bhi", [P, KD, SEQ], f32r)
        blo = sb("blo", [P, KD, SEQ], f32r)
        kxT = sb("kxT", [P, NXH, SEQ])
        vx = sb("vx", [P, TT, XW])
        proj_at = place[0]
        proj = sb("proj", [P, TT, G_OUT * GC - G_V * GC])
        mask = sb("mask", [P, 3 * P])
        cos = sb("cos", [P, TT, 2, HD // 2])
        sin = sb("sin", [P, TT, 2, HD // 2])
        probs = sb("probs", [P, 3 * P])
        probsT = sb("probsT", [P, 3 * P])
        masked = sb("masked", [P, 3 * P])
        osc = sb("osc", [P, TT, HD])
        small = sb("small", [P, 16, TT])
        mx, negm, den, rden, rden2, oss, ovar, orstd, oscale = (small[:, n, :] for n in range(9))
        conv_at = [place[0]]
        qkr = sb("qkr", [P, 2, TT, 2, HD])
        rtmp = sb("rtmp", [P, 4, TT, 2, HD // 2])
        qkT = sb("qkT", [P, 4, P])
        assert place[0] <= nc.sbuf_usable_end, (place[0], nc.sbuf_usable_end)
        uT = sb("uT", [P, 2, 2 + SEQ], at=conv_at)
        cy = sb("cy", [P, 4, SEQ], at=conv_at)
        csq = sb("csq", [P, 4, SEQ], at=conv_at)
        place[0] = max(place[0], conv_at[0])
        assert place[0] <= nc.sbuf_usable_end, (place[0], nc.sbuf_usable_end)
        memx = proj[:, :, 0:D]
        junk0 = proj[:, 0, D:2 * D]
        kx = proj[:, :, 2 * D:2 * D + XW]
        prep_at = [proj_at + 4 * (2 * D + XW)]
        parr = sb("parr", [NPAR, P], at=prep_at)
        posi = sb("posi", [P, TT], i32, at=prep_at)
        posf = sb("posf", [P, TT], at=prep_at)
        invf = sb("invf", [P, HD // 2], at=prep_at)
        ang, kk, kh, kl, red, cred, wrap = (sb(n, [P, TT, HD // 2], at=prep_at)
                                            for n in ("ang", "kk", "kh", "kl", "red", "cred", "wrap"))
        assert prep_at[0] <= proj_at + 4 * (G_OUT - G_V) * GC
        xat = [proj_at]
        q2 = sb("q2", [P, TT, XW], at=xat)
        q2T = sb("q2T", [P, NXH, SEQ], at=xat)
        xp = sb("xp", [P, NXH, TT, SEQ], at=xat)
        xpT = sb("xpT", [P, NXH, TT, SEQ], at=xat)
        oxhi = sb("oxhi", [P, NXH, SEQ], f32r, at=xat)
        oxlo = sb("oxlo", [P, NXH, SEQ], f32r, at=xat)
        xsm = sb("xsm", [P, 4, NXH, TT], at=xat)
        xmx, xnegm, xden, xrd = (xsm[:, n] for n in range(4))
        junk1 = sb("junk1", [P, D], at=xat)
        fat = [shared]
        fhi = sb("fhi", [P, FF // P, SEQ], f32r, at=fat)
        flo = sb("flo", [P, FF // P, SEQ], f32r, at=fat)
        silu = sb("silu", [P, TT, GC], at=fat)
        fact = sb("fact", [P, TT, GC], at=fat)
        gfin = sb("gfin", [P, D], at=fat)
        junk2 = sb("junk2", [P, GC], at=fat)
        assert fat[0] <= nc.sbuf_usable_end, (fat[0], nc.sbuf_usable_end)
        ps = ctx.enter_context(nc.psum_tensor("ps", [P, 8, GC], f32))

        w_loaded = [sem(f"w_loaded{s}") for s in range(RING)]
        hi_ready = sem("hi_ready")
        lo_ready = sem("lo_ready")
        step_used = sem("step_used")
        evacuated = [sem("even_evacuated"), sem("odd_evacuated")]
        mem_loaded = [sem(f"mem_loaded{c}") for c in range(4)]
        x_loaded = [sem(f"x_loaded{c}") for c in range(4)]
        par_loaded, pos_loaded, gfin_loaded = sem("par_loaded"), sem("pos_loaded"), sem("gfin_loaded")
        blank, consts_ready = sem("blank"), sem("consts_ready")
        par_T, par_ready = sem("par_T"), sem("par_ready")
        unit_T, unit_hi, unit_lo = sem("unit_T"), sem("unit_hi"), sem("unit_lo")
        squares, var_ready, rstd_ready = sem("squares"), sem("var_ready"), sem("rstd_ready")
        table_step, angles_ready, table_ready = sem("table_step"), sem("angles_ready"), sem("table_ready")
        kx_T, kxT_ready = sem("kx_T"), sem("kxT_ready")
        rope_products, rope_done = sem("rope_products"), sem("rope_done")
        qk_T, qkT_ready = sem("qk_T"), sem("qkT_ready")
        scores_ready, scores_masked = sem("scores_ready"), sem("scores_masked")
        max_ready, negmax_ready = sem("max_ready"), sem("negmax_ready")
        probs_ready, probs_T, probsT_ready = sem("probs_ready"), sem("probs_T"), sem("probsT_ready")
        pv_ready, o_squares, den_step = sem("pv_ready"), sem("o_squares"), sem("den_step")
        o_var, o_rstd, o_scale, o_scaled = sem("o_var"), sem("o_rstd"), sem("o_scale"), sem("o_scaled")
        o_T, merged_hi, merged_attn = sem("o_T"), sem("merged_hi"), sem("merged_attn")
        u_ready, conv_T, conv_u = sem("u_ready"), sem("conv_T"), sem("conv_u")
        conv_tap, conv_y, conv_sq = sem("conv_tap"), sem("conv_y"), sem("conv_sq")
        conv_ss, conv_root, conv_rec = sem("conv_ss"), sem("conv_root"), sem("conv_rec")
        conv_norm, conv_hi, merged_conv = sem("conv_norm"), sem("conv_hi"), sem("merged_conv")
        pad_ready = sem("pad_ready")
        q2_T, q2T_ready = sem("q2_T"), [sem("q2T_by_act"), sem("q2T_by_dve")]
        xs_ready, xmax, xneg, xexp = sem("xs_ready"), sem("xmax"), sem("xneg"), sem("xexp")
        xrec, xnorm, xp_T = sem("xrec"), sem("xnorm"), sem("xp_T")
        xpT_ready = [sem("xpT_by_act"), sem("xpT_by_dve")]
        xo_ready, xo_hi, xo_lo = sem("xo_ready"), sem("xo_hi"), sem("xo_lo")
        part_ready, fsum_ready, fvar_ready, frstd_ready = (
            sem(n) for n in ("part_ready", "fsum_ready", "fvar_ready", "frstd_ready"))
        gained = sem("gained")
        final_ready, stored = [sem("final_by_act"), sem("final_by_dve")], sem("stored")

        block = ctx.enter_context(nc.Block())

        def tile_pair(buf, j):
            return buf[:, j % RING, :]

        def loaded_by(j, it):
            return 16 * (j // RING + 1) + it * (16 // RING)

        def await_out(eng, g, gi=0):
            eng.wait_ge(evacuated[g % 2], gi + (g // 2 + 1))

        def gain(col):
            return par[:, ds(col, 1)]

        def unit_bank(u):
            return 4 + u % 4 if u < U_H2 else 6 + u % 2

        @block.sync
        def _(sp):
            for c in range(4):
                sp.dma_start(memx[:, :, c * GC:(c + 1) * GC],
                             mem[:, c * GC:(c + 1) * GC].rearrange("(t p) d -> p t d", p=P)).then_inc(mem_loaded[c], 16)
            for s in range(RING):
                sp.dma_start(tile_pair(raw, s), stream[s]).then_inc(w_loaded[s], 16)
            with sp.Fori(1, STEPS // RING) as i:
                for s in range(RING):
                    sp.wait_ge(lo_ready, i * RING + (s - RING + 1))
                    sp.dma_start(tile_pair(raw, s), stream[i * RING + s]).then_inc(w_loaded[s], 16)
            for n in range(TT * 2):
                t, h = n % 2, n // 2
                sp.wait_ge(final_ready[t], h + 1)
                sp.dma_start(out[t * P:(t + 1) * P, h * (D // 2):(h + 1) * (D // 2)],
                             yout[:, t, h * (D // 2):(h + 1) * (D // 2)]).then_inc(stored, 16)
            sp.wait_ge(stored, 16 * TT * 2)

        @block.gpsimd
        def _(pool):
            pool.memset(ident[:], 0.0).then_inc(blank, 1)
            pool.memset(mask[:], 0.0).then_inc(blank, 1)
            pool.memset(ones[:], 1.0).then_inc(consts_ready, 1)
            pool.memset(eps[:], EPS).then_inc(consts_ready, 1)
            pool.memset(mhalf[:], -0.5).then_inc(consts_ready, 1)
            pool.wait_ge(blank, 2)
            pool.affine_select(out=ident[:], in_=ident[:], compare_op=ALU.not_equal, fill=1.0, base=0,
                               pattern=[[-1, P]], channel_multiplier=1).then_inc(consts_ready, 1)
            for n in (0, 2):
                pool.affine_select(out=mask[:, n * P:(n + 1) * P], in_=mask[:, n * P:(n + 1) * P],
                                   compare_op=ALU.is_ge, fill=MASKED, base=0,
                                   pattern=[[-1, P]], channel_multiplier=1).then_inc(consts_ready, 1)

            def root(n):
                pool.wait_ge(var_ready, n + 1)
                nc.gpsimd.tensor_tensor(rstd[:, n, :], vpe[:, n, :], mhalf[:], ALU.pow).then_inc(rstd_ready, 1)

            def rope(h, parity):
                src = proj[:, :, ds(AW + h * (2 * HD), 2 * HD)].rearrange("p t (q f) -> p t q f", q=2)
                lo_half, hi_half = src[:, :, :, 0:HD // 2], src[:, :, :, HD // 2:HD]
                pool.wait_ge(rope_done, 2 * h)
                for n, (a, b) in enumerate(((lo_half, cos), (hi_half, sin), (hi_half, cos), (lo_half, sin))):
                    nc.gpsimd.tensor_tensor(rtmp[:, n], a, b[:], ALU.mult).then_inc(rope_products, 1)
                pool.wait_ge(rope_products, 4 * h + 4)
                dst = qkr[:, parity]
                nc.gpsimd.tensor_tensor(dst[:, :, :, 0:HD // 2], rtmp[:, 0], rtmp[:, 1], ALU.subtract).then_inc(rope_done, 1)
                nc.gpsimd.tensor_tensor(dst[:, :, :, HD // 2:HD], rtmp[:, 2], rtmp[:, 3], ALU.add).then_inc(rope_done, 1)

            def head_root(h):
                pool.wait_ge(o_var, h + 1)
                nc.gpsimd.tensor_tensor(orstd, ovar, mhalf[:], ALU.pow).then_inc(o_rstd, 1)

            pool.wait_ge(consts_ready, 3)
            root(0)
            root(1)
            pool.wait_ge(table_ready, 4)
            await_out(pool, G_QK)
            rope(0, 0)
            rope(1, 1)
            with pool.Fori(0, NH // 2 - 1) as i:
                for n in range(2):
                    h = i * 2 + n
                    head_root(h)
                    pool.wait_ge(qk_T, h + 1)
                    rope(h + 2, n)
            head_root(NH - 2)
            head_root(NH - 1)
            c0, x0 = (G_C - G_V) * GC, (G_X - G_V) * GC
            for n in range(2):
                await_out(pool, G_X + n)
                u = proj[:, :, x0 + n * GC:x0 + (n + 1) * GC]
                nc.gpsimd.tensor_tensor(u, proj[:, :, c0 + n * GC:c0 + (n + 1) * GC], u, ALU.mult).then_inc(u_ready, 1)
            root(2)
            root(3)
            pool.wait_ge(fvar_ready, 1)
            nc.gpsimd.tensor_tensor(frstd[:], fvar[:], mhalf[:], ALU.pow).then_inc(frstd_ready, 1)

        @block.tensor
        def _(pe):
            def step(j, it, k, hi, lo, parity, first, last):
                pe.wait_ge(lo_ready, it + (j + 1))
                for n in range(KS):
                    w_h, w_l = (tile_pair(b, j)[:, n * GC:(n + 1) * GC] for b in (whi, wlo))
                    for t in range(TT):
                        a_h, a_l = (b[:, k + n, t * P:(t + 1) * P] for b in (hi, lo))
                        bank = ps[:, 2 * parity + t, :]
                        nc.tensor.matmul(bank, lhsT=a_h, rhs=w_h, start=first and n == 0, stop=False)
                        nc.tensor.matmul(bank, lhsT=a_h, rhs=w_l, start=False, stop=False)
                        done = nc.tensor.matmul(bank, lhsT=a_l, rhs=w_h, start=False, stop=last and n == KS - 1)
                done.then_inc(step_used, 1)

            def bank_free(g, gi=0):
                if g >= 2:
                    pe.wait_ge(evacuated[g % 2], gi + (g // 2))

            def group_step(g, s, hi, lo, it=0, gi=0, n_steps=SPG, j0=None):
                j = (g * SPG if j0 is None else j0) + s
                if s == 0:
                    bank_free(g, gi)
                step(j, it, KS * s, hi, lo, g % 2, s == 0, s == n_steps - 1)

            def unit(u, src, k, ui=0):
                bank = ps[:, unit_bank(u), :].rearrange("p (k t) -> p k t", k=KS)
                for n in range(KS):
                    for t in range(TT):
                        done = nc.tensor.transpose(bank[:, n, t * P:(t + 1) * P],
                                                   src[:, t, (k + n) * P:(k + n + 1) * P], ident[:])
                done.then_inc(unit_T, 1)

            pe.wait_ge(consts_ready, 6)
            pe.wait_ge(par_loaded, 16)
            nc.tensor.transpose(ps[:, 0, 0:NPAR], parr[:], ident[0:NPAR, 0:NPAR]).then_inc(par_T, 1)
            for u in range(SPG):
                if u % 2 == 0:
                    pe.wait_ge(mem_loaded[u // 2], 16)
                if u >= 4:
                    pe.wait_ge(unit_lo, u - 3)
                unit(U_MEM + u, memx, KS * u)
            pe.wait_ge(par_ready, 1)
            for g in (G_KV, G_KV + 1):
                for s in range(SPG):
                    n = g * SPG + s
                    if n % 2 == 0:
                        u = n // 2
                        if u % 2 == 0:
                            pe.wait_ge(x_loaded[u // 2], 16)
                        pe.wait_ge(unit_lo, U_X + u - 3)
                        unit(U_X + u, res, KS * u)
                    if g == G_KV:
                        pe.wait_ge(unit_lo, U_MEM + s + 1)
                    group_step(g, s, ahi, alo)
            pe.wait_ge(unit_lo, U_X + SPG)
            for g in range(G_V, G_QK + 2):
                for s in range(SPG if g <= G_QK else 3):
                    if g == G_V and s == 1:
                        await_out(pe, G_KV)
                        for h in range(NXH):
                            for t in range(TT):
                                done = nc.tensor.transpose(ps[:, 4 + h // 2, ((h % 2) * TT + t) * P:((h % 2) * TT + t + 1) * P],
                                                           kx[:, t, h * HD:(h + 1) * HD], ident[:])
                        done.then_inc(kx_T, 1)
                    group_step(g, s, bhi, blo)
            pe.wait_ge(kxT_ready, 1)

            def head_front(h, parity, stage):
                if stage == 0:
                    pe.wait_ge(rope_done, 2 * h + 2)
                    pe.wait_ge(scores_masked, h + 0)
                    for n in range(4):
                        done = nc.tensor.transpose(ps[:, 4, n * P:(n + 1) * P], qkr[:, parity, n % 2, n // 2, :], ident[:])
                    done.then_inc(qk_T, 1)
                if stage == 2:
                    pe.wait_ge(qkT_ready, h + 1)
                    nc.tensor.matmul(ps[:, 4, 0:P], lhsT=qkT[:, 0, :], rhs=qkT[:, 2, :], start=True, stop=True)
                    nc.tensor.matmul(ps[:, 4, P:3 * P], lhsT=qkT[:, 1, :], rhs=qkT[:, 2:4, :].rearrange("p a b -> p (a b)"),
                                     start=True, stop=True).then_inc(scores_ready, 1)
                if stage == 4:
                    pe.wait_ge(probs_ready, h + 1)
                    pe.wait_ge(merged_attn, h + 0)
                    for n in range(3):
                        done = nc.tensor.transpose(ps[:, 5, n * P:(n + 1) * P], probs[:, n * P:(n + 1) * P], ident[:])
                    done.then_inc(probs_T, 1)
                if stage == 5:
                    pe.wait_ge(probsT_ready, h + 1)
                    v0, v1 = (proj[:, t, ds(h * HD, HD)] for t in range(TT))
                    nc.tensor.matmul(ps[:, 5, 0:P], lhsT=probsT[:, 0:P], rhs=v0, start=True, stop=True)
                    nc.tensor.matmul(ps[:, 5, P:2 * P], lhsT=probsT[:, P:2 * P], rhs=v0, start=True, stop=False)
                    nc.tensor.matmul(ps[:, 5, P:2 * P], lhsT=probsT[:, 2 * P:3 * P], rhs=v1,
                                     start=False, stop=True).then_inc(pv_ready, 1)
                if stage == 7:
                    pe.wait_ge(o_scaled, h + 1)
                    for t in range(TT):
                        done = nc.tensor.transpose(ps[:, 5, (2 + t) * P:(3 + t) * P], osc[:, t, :], ident[:])
                    done.then_inc(o_T, 1)

            with pe.Fori(0, NH // 2) as i:
                for n in range(2):
                    for r in range(SPG):
                        head_front(i * 2 + n, n, r)
                        s = (3 + r) % SPG
                        g = G_QK + 1 + n + (3 + r) // SPG
                        group_step(g, s, bhi, blo, it=i * (2 * SPG), gi=i)

            def conv_front(b):
                pe.wait_ge(u_ready, b // 4 + 1)
                bank = CONV_BANKS[b % 4]
                if b == 3:
                    pe.wait_ge(merged_attn, NH)
                if b >= 4:
                    pe.wait_ge(conv_root, b - 3)
                for n, c in enumerate(((G_X - G_V) * GC, (G_X - G_V) * GC - CW)):
                    for t in range(TT):
                        done = nc.tensor.transpose(ps[:, bank, (n * TT + t) * P:(n * TT + t + 1) * P],
                                                   proj[:, t, c + b * P:c + (b + 1) * P], ident[:])
                done.then_inc(conv_T, 1)

            def conv_sums(b):
                pe.wait_ge(conv_sq, b + 1)
                nc.tensor.matmul(ps[:, CONV_BANKS[b % 4], 0:SEQ], lhsT=ones[:], rhs=csq[:, b % 4, :],
                                 start=True, stop=True).then_inc(conv_ss, 1)

            for s in range(3, SPG):
                for b in {3: (0, 1), 4: (2, 3)}.get(s, ()):
                    conv_front(b)
                for b in {6: (0, 1), 7: (2, 3)}.get(s, ()):
                    conv_sums(b)
                group_step(G_X + 1, s, bhi, blo)
            for g in range(G_OUT, G_XQ):
                for s in range(SPG):
                    if g == G_OUT:
                        for b in {2: (4, 5), 3: (6, 7)}.get(s, ()):
                            conv_front(b)
                        for b in {5: (4, 5), 6: (6, 7)}.get(s, ()):
                            conv_sums(b)
                        if s < NH // KS:
                            pe.wait_ge(merged_attn, KS * (s + 1))
                        else:
                            pe.wait_ge(merged_conv, KS * (s - NH // KS + 1))
                    elif s in (1, 2):
                        u = 2 * (g - G_OUT - 1) + s - 1
                        await_out(pe, g - 1)
                        if u == 0 or u == 1:
                            pe.wait_ge(merged_conv, CB)
                        pe.wait_ge(unit_lo, U_H2 + u - 1)
                        unit(U_H2 + u, res, KS * u)
                    group_step(g, s, ahi, alo)
            for s in range(SPG):
                if s in (1, 2):
                    u = 2 * (D // GC - 1) + s - 1
                    await_out(pe, G_XQ - 1)
                    pe.wait_ge(unit_lo, U_H2 + u - 1)
                    unit(U_H2 + u, res, KS * u)
                pe.wait_ge(unit_lo, U_H2 + s + 1)
                group_step(G_XQ, s, bhi, blo)
            await_out(pe, G_XQ)
            for h in range(NXH):
                for t in range(TT):
                    done = nc.tensor.transpose(ps[:, 6 + h // 2, ((h % 2) * TT + t) * P:((h % 2) * TT + t + 1) * P],
                                               q2[:, t, h * HD:(h + 1) * HD], ident[:])
                if h % 2:
                    done.then_inc(q2_T, 1)
            for h in range(NXH):
                if h % 2 == 0:
                    pe.wait_ge(q2T_ready[h // 2], 1)
                for t in range(TT):
                    done = nc.tensor.matmul(ps[:, 4 + h, t * SEQ:(t + 1) * SEQ], lhsT=q2T[:, h, t * P:(t + 1) * P],
                                            rhs=kxT[:, h, :], start=True, stop=True)
                done.then_inc(xs_ready, 1)
            for h in range(NXH):
                pe.wait_ge(xnorm, TT * (h + 1))
                for m in range(TT):
                    for t in range(TT):
                        done = nc.tensor.transpose(ps[:, 4 + h, (m * TT + t) * P:(m * TT + t + 1) * P],
                                                   xp[:, h, t, m * P:(m + 1) * P], ident[:])
                done.then_inc(xp_T, 1)
            for h in range(NXH):
                pe.wait_ge(xpT_ready[h % 2], h // 2 + 1)
                for m in range(TT):
                    done = nc.tensor.matmul(ps[:, 4 + h, 0:SEQ], lhsT=vx[:, m, h * HD:(h + 1) * HD], rhs=xpT[:, h, m, :],
                                            start=m == 0, stop=m == TT - 1)
                done.then_inc(xo_ready, 1)
            for g in range(G_XO, G_FF):
                for s in range(SXO):
                    if g > G_XO and s == 1:
                        await_out(pe, g - 1)
                        for u in (2 * (g - G_XO - 1), 2 * (g - G_XO - 1) + 1):
                            pe.wait_ge(unit_lo, U_H3 + u - 1)
                            unit(U_H3 + u, res, KS * u)
                    if g == G_XO:
                        pe.wait_ge(xo_lo, KS * (s + 1))
                    group_step(g, s, oxhi, oxlo, n_steps=SXO, j0=J_XO + SXO * (g - G_XO))

            def chunk(c, ci=0):
                for half in range(2):
                    for s in range(SPG):
                        if half == 0 and c == 0 and s == 1:
                            await_out(pe, G_FF - 1)
                            for u in (SPG - 2, SPG - 1):
                                pe.wait_ge(unit_lo, U_H3 + u - 1)
                                unit(U_H3 + u, res, KS * u)
                        if half == 0 and c == 0:
                            pe.wait_ge(unit_lo, U_H3 + s + 1)
                        if half == 0 and c == 1 and s in (2, 3):
                            ffn_unit(s - 2, ci)
                        group_step(G_FF + 2 * c + half, s, ahi, alo, it=ci * (2 * SPG), gi=ci,
                                   j0=J_FF + (2 * c + half) * SPG)

            def ffn_unit(n, ci):
                await_out(pe, G_FF + 1, ci)
                pe.wait_ge(unit_lo, ci * 2 + (U_FF + n - 1))
                unit(U_FF + n, fact, KS * n)

            chunk(0)
            with pe.Fori(0, NFC - 1) as ci:
                chunk(1, ci)
            ffn_unit(0, NFC - 1)
            ffn_unit(1, NFC - 1)
            pe.wait_ge(unit_lo, U_FF + 2 * NFC)
            with pe.Fori(0, D // GC // 2) as i:
                for n in range(2):
                    for s in range(SDN):
                        group_step(G_DN + n, s, fhi, flo, it=i * (2 * SDN), gi=i, n_steps=SDN, j0=J_DN + n * SDN)

        @block.scalar
        def _(act):
            act.dma_start(parr[:], params).then_inc(par_loaded, 16)
            act.dma_start(posi[:], pos).then_inc(pos_loaded, 16)
            act.dma_start(invf[:], inv_freq).then_inc(pos_loaded, 16)
            for c in range(4):
                act.dma_start(res[:, :, c * GC:(c + 1) * GC],
                              x[:, c * GC:(c + 1) * GC].rearrange("(t p) d -> p t d", p=P)).then_inc(x_loaded[c], 16)

            def cast(j, it=0):
                if isinstance(it, int) and j >= STEPS:
                    return
                act.wait_ge(w_loaded[j % RING], loaded_by(j, it))
                if j >= RING:
                    act.wait_ge(step_used, it + (j - RING + 1))
                nc.scalar.activation(tile_pair(whi, j), tile_pair(raw, j), ACT.Copy).then_inc(hi_ready, 1)

            def unit(u, k, col, hi, ui=0, uk=0):
                act.wait_ge(unit_T, ui + (u + 1))
                bank = ps[:, unit_bank(u), :].rearrange("p (k t) -> p k t", k=KS)
                if col is None:
                    done = nc.scalar.activation(hi[:, ds(uk + k, KS), :], bank, ACT.Copy)
                else:
                    for n in range(KS):
                        done = nc.scalar.activation(hi[:, k + n, :], bank[:, n, :], ACT.Copy, scale=gain(col + k + n))
                done.then_inc(unit_hi, 1)

            def sum_squares(n, src, junk):
                for t in range(TT):
                    if n or t:
                        act.wait_ge(squares, TT * n + t)
                    nc.scalar.activation(junk, src[:, t, :], ACT.Square, accum_out=ssq[:, n, t:t + 1]).then_inc(squares, 1)

            def evacuate(g, end, dst, scale, gi=0, steps=0, func=ACT.Copy):
                act.wait_ge(step_used, steps + end)
                for t in range(TT):
                    done = nc.scalar.activation(dst(t), ps[:, 2 * (g % 2) + t, :], func, scale=scale(t))
                done.then_inc(evacuated[g % 2], 1)

            for j in range(LEAD):
                cast(j)
            act.wait_ge(par_ready, 1)
            for u in range(SPG):
                unit(U_MEM + u, KS * u, C_MEM, ahi)
            for j in range(G_V * SPG):
                cast(j + LEAD)
                if j == SPG:
                    act.wait_ge(rstd_ready, 1)
                    evacuate(G_KV, j, lambda t: kx[:, t, :], lambda t: rstd[:, 0, t:t + 1])
                if j % 2 == 0:
                    unit(U_X + j // 2, j, C_MIX, bhi)
                if j == 1:
                    sum_squares(0, memx, junk0)
                if j == SPG + 1:
                    for c in range(4):
                        act.wait_ge(x_loaded[c], 16)
                    sum_squares(1, res, junk0)

            def project(g, i=0):
                evacuate(g, SPG * (g + 1), lambda t: proj[:, t, ds(i * (2 * GC) + (g - G_V) * GC, GC)],
                         lambda t: rstd[:, 1, t:t + 1], gi=i, steps=i * (2 * SPG))

            for j in range(G_V * SPG, (G_QK + 1) * SPG + 3):
                g, s = divmod(j, SPG)
                cast(j + LEAD)
                if s == 0 and g == G_V:
                    evacuate(G_KV + 1, j, lambda t: vx[:, t, :], lambda t: rstd[:, 0, t:t + 1])
                if s == 1 and g == G_V:
                    act.wait_ge(kx_T, 1)
                    for n in range(NXH // 2):
                        done = nc.scalar.activation(kxT[:, 2 * n:2 * n + 2, :].rearrange("p a b -> p (a b)"),
                                                    ps[:, 4 + n, :], ACT.Copy)
                    done.then_inc(kxT_ready, 1)
                if s == 0 and g > G_V:
                    if g == G_V + 1:
                        act.wait_ge(rstd_ready, 2)
                    project(g - 1)
                if s == 4 and g == G_V + 1:
                    act.wait_ge(angles_ready, 2)
                    for table, angle in ((sin, red), (cos, cred)):
                        for q in range(2):
                            nc.scalar.activation(table[:, :, q, :], angle[:], ACT.Sin).then_inc(table_ready, 1)

            def head(h, r):
                if r == 0:
                    act.wait_ge(qk_T, h + 1)
                    act.wait_ge(scores_ready, h + 0)
                    nc.scalar.activation(qkT[:].rearrange("p a b -> p (a b)"), ps[:, 4, :], ACT.Copy).then_inc(qkT_ready, 1)
                if r == 3:
                    act.wait_ge(negmax_ready, h + 1)
                    act.wait_ge(probs_T, h + 0)
                    nc.scalar.activation(probs[:, 0:P], masked[:, 0:P], ACT.Exp, bias=negm[:, 0:1], scale=SCALE,
                                         accum_out=den[:, 0:1])
                    nc.scalar.activation(probs[:, P:3 * P], masked[:, P:3 * P], ACT.Exp, bias=negm[:, 1:2], scale=SCALE,
                                         accum_out=den[:, 1:2]).then_inc(probs_ready, 1)
                if r == 5:
                    act.wait_ge(pv_ready, h + 1)
                    for t in range(TT):
                        if t:
                            act.wait_ge(o_squares, 2 * h + 1)
                        nc.scalar.activation(osc[:, 0, :], ps[:, 5, t * HD:(t + 1) * HD], ACT.Square,
                                             accum_out=oss[:, t:t + 1]).then_inc(o_squares, 1)
                if r == 7:
                    act.wait_ge(o_T, h + 1)
                    nc.scalar.activation(ahi[:, ds(h, 1), :].rearrange("p a b -> p (a b)"), ps[:, 5, 2 * P:4 * P],
                                         ACT.Copy, scale=gain(C_ATTN + h)).then_inc(merged_hi, 1)

            with act.Fori(0, NH // 2) as i:
                for n in range(2):
                    for r in range(SPG):
                        j = (G_QK + 1 + n) * SPG + 3 + r
                        cast(j + LEAD, i * (2 * SPG))
                        if r == 5:
                            project(G_QK + 1 + n, i)
                        head(i * 2 + n, r)

            def conv_in(b):
                act.wait_ge(conv_T, b + 1)
                if b == 0:
                    act.wait_ge(pad_ready, 1)
                if b >= 2:
                    act.wait_ge(conv_tap, 2 * (b - 1))
                if b >= 4:
                    act.wait_ge(merged_conv, b - 3)
                u = ps[:, CONV_BANKS[b % 4], 0:SEQ]
                nc.scalar.activation(uT[:, b % 2, 2:2 + SEQ], u, ACT.Copy)
                nc.scalar.activation(cy[:, b % 4, :], u, ACT.Identity, bias=gain(C_BC + b),
                                     scale=gain(C_WC + 2 * CB + b)).then_inc(conv_u, 1)

            def conv_square(b):
                act.wait_ge(conv_y, b + 1)
                if b >= 4:
                    act.wait_ge(conv_norm, b - 3)
                nc.scalar.activation(csq[:, b % 4, :], cy[:, b % 4, :], ACT.Square).then_inc(conv_sq, 1)

            def conv_sqrt(b):
                act.wait_ge(conv_ss, b + 1)
                nc.scalar.activation(csq[:, b % 4, :], ps[:, CONV_BANKS[b % 4], 0:SEQ], ACT.Sqrt, bias=eps[:],
                                     scale=1.0 / HD).then_inc(conv_root, 1)

            def conv_out(b):
                act.wait_ge(conv_norm, b + 1)
                nc.scalar.activation(ahi[:, NH + b, :], cy[:, b % 4, :], ACT.Copy).then_inc(conv_hi, 1)

            for j in range((G_X + 1) * SPG + 3, G_XQ * SPG + SPG):
                g, s = divmod(j, SPG)
                cast(j + LEAD)
                if g == G_X + 1:
                    for b in {3: (0, 1), 4: (2, 3)}.get(s, ()):
                        conv_in(b)
                    for b in {4: (0, 1), 5: (2, 3)}.get(s, ()):
                        conv_square(b)
                    for b in {6: (0, 1), 7: (2, 3)}.get(s, ()):
                        conv_sqrt(b)
                    if s == 7:
                        conv_out(0)
                        conv_out(1)
                if g == G_OUT:
                    if s == 0:
                        project(G_X + 1)
                        conv_out(2)
                        conv_out(3)
                    for b in {2: (4, 5), 3: (6, 7)}.get(s, ()):
                        conv_in(b)
                    for b in {3: (4, 5), 4: (6, 7)}.get(s, ()):
                        conv_square(b)
                    for b in {5: (4, 5), 6: (6, 7)}.get(s, ()):
                        conv_sqrt(b)
                    for b in {5: (4, 5), 6: (6, 7)}.get(s, ()):
                        conv_out(b)
                if g > G_OUT and s in (1, 2):
                    u = 2 * (g - G_OUT - 1) + s - 1
                    unit(U_H2 + u, KS * u, C_XATTN, bhi)
                if g == G_XQ and s == 3:
                    await_out(act, G_XQ - 1)
                    sum_squares(2, res, junk1[:])
            j = J_XO
            cast(j + LEAD)
            act.wait_ge(rstd_ready, 3)
            evacuate(G_XQ, J_XO, lambda t: q2[:, t, :], lambda t: rstd[:, 2, t:t + 1])
            act.wait_ge(q2_T, 1)
            nc.scalar.activation(q2T[:, 0:2, :].rearrange("p a b -> p (a b)"), ps[:, 6, :], ACT.Copy).then_inc(q2T_ready[0], 1)
            for h in range(NXH):
                act.wait_ge(xneg, h + 1)
                for t in range(TT):
                    nc.scalar.activation(xp[:, h, t, :], ps[:, 4 + h, t * SEQ:(t + 1) * SEQ], ACT.Exp,
                                         bias=xnegm[:, h, t:t + 1], scale=SCALE,
                                         accum_out=xden[:, h, t:t + 1]).then_inc(xexp, 1)
            for h in range(0, NXH, 2):
                act.wait_ge(xp_T, h + 1)
                nc.scalar.activation(xpT[:, h].rearrange("p a b -> p (a b)"), ps[:, 4 + h, :], ACT.Copy).then_inc(xpT_ready[0], 1)
            for h in range(NXH):
                act.wait_ge(xo_ready, h + 1)
                nc.scalar.activation(oxhi[:, h, :], ps[:, 4 + h, 0:SEQ], ACT.Copy).then_inc(xo_hi, 1)
            for j in range(J_XO + 1, J_FF):
                cast(j + LEAD)
                if (j - J_XO) % SXO == 1 and j - J_XO > SXO:
                    for n in range(2):
                        u = 2 * ((j - J_XO) // SXO - 1) + n
                        unit(U_H3 + u, KS * u, C_FFN, ahi)

            def gate(c, ci=0):
                if isinstance(ci, int) and c == 0:
                    act.wait_ge(rstd_ready, 4)
                else:
                    await_out(act, G_FF + 2 * c - 1, ci)
                evacuate(G_FF + 2 * c, J_FF + (2 * c + 1) * SPG, lambda t: silu[:, t, :], lambda t: rstd[:, 3, t:t + 1],
                         gi=ci, steps=ci * (2 * SPG), func=ACT.Silu)

            for s in range(2 * SPG):
                j = J_FF + s
                cast(j + LEAD)
                if s == 1:
                    for u in (SPG - 2, SPG - 1):
                        unit(U_H3 + u, KS * u, C_FFN, ahi)
                if s == 2:
                    await_out(act, G_FF - 1)
                    sum_squares(3, res, junk1[:])
                if s == SPG:
                    gate(0)
            act.dma_start(gfin[:], g_final.partition_broadcast(P)).then_inc(gfin_loaded, 16)
            with act.Fori(0, NFC - 1) as ci:
                for s in range(2 * SPG):
                    cast(J_FF + 2 * SPG + s + LEAD, ci * (2 * SPG))
                    if s in (2, 3):
                        unit(U_FF + s - 2, KS * (s - 2), None, fhi, ui=ci * 2, uk=ci * (2 * KS))
                    if s == SPG:
                        gate(1, ci)
            for n in range(2):
                unit(U_FF + 2 * (NFC - 1) + n, 2 * KS * (NFC - 1) + KS * n, None, fhi)

            def result_squares(g):
                await_out(act, G_DN + g)
                for t in range(TT):
                    if g or t:
                        act.wait_ge(part_ready, TT * g + t)
                    nc.scalar.activation(junk2[:], res[:, t, g * GC:(g + 1) * GC], ACT.Square,
                                         accum_out=part[:, t, g:g + 1]).then_inc(part_ready, 1)

            for g in range(D // GC):
                for s in range(SDN):
                    cast(J_DN + g * SDN + s + LEAD)
                    if g and s == 1:
                        result_squares(g - 1)
            result_squares(D // GC - 1)
            act.wait_ge(frstd_ready, 1)
            act.wait_ge(gained, TT * (D // GC))
            for h in range(2):
                part_of = slice(h * (D // 2), (h + 1) * (D // 2))
                nc.scalar.activation(yout[:, 0, part_of], yout[:, 0, part_of], ACT.Copy,
                                     scale=frstd[:, 0:1]).then_inc(final_ready[0], 1)

        @block.vector
        def _(dve):
            vec = nc.vector

            def split(j, it=0):
                if isinstance(it, int) and j >= STEPS:
                    return
                dve.wait_ge(hi_ready, it + (j + 1))
                vec.tensor_tensor(tile_pair(wlo, j), tile_pair(raw, j), tile_pair(whi, j).bitcast(f32),
                                  ALU.subtract).then_inc(lo_ready, 1)

            def unit(u, k, col, hi, lo, ui=0, uk=0):
                dve.wait_ge(unit_hi, ui + (u + 1))
                bank = ps[:, unit_bank(u), :].rearrange("p (k t) -> p k t", k=KS)
                if col is None:
                    here = ds(uk + k, KS)
                    done = vec.tensor_tensor(lo[:, here, :], bank, hi[:, here, :].bitcast(f32), ALU.subtract)
                else:
                    for n in range(KS):
                        done = vec.scalar_tensor_tensor(lo[:, k + n, :], bank[:, n, :], gain(col + k + n),
                                                        hi[:, k + n, :].bitcast(f32), ALU.mult, ALU.subtract)
                done.then_inc(unit_lo, 1)

            def variance(n):
                dve.wait_ge(squares, TT * (n + 1))
                vec.tensor_scalar(vpe[:, n, :], ssq[:, n, :], 1.0 / D, EPS, ALU.mult, ALU.add).then_inc(var_ready, 1)

            def add_group(g, end):
                first = G_DN if g >= G_DN else G_XO if g >= G_XO else G_OUT
                dve.wait_ge(step_used, end)
                for t in range(TT):
                    cols = res[:, t, (g - first) * GC:(g - first + 1) * GC]
                    done = vec.tensor_tensor(cols, ps[:, 2 * (g % 2) + t, :], cols, ALU.add)
                done.then_inc(evacuated[g % 2], 1)

            dve.wait_ge(par_T, 1)
            vec.tensor_copy(par[:], ps[:, 0, 0:NPAR]).then_inc(par_ready, 1)
            for j in range(LEAD):
                split(j)
            dve.wait_ge(par_ready, 1)
            for u in range(SPG):
                unit(U_MEM + u, KS * u, C_MEM, ahi, alo)
            for j in range(G_V * SPG):
                split(j + LEAD)
                if j % 2 == 0:
                    unit(U_X + j // 2, j, C_MIX, bhi, blo)
                if j == 3:
                    variance(0)
                if j == SPG + 3:
                    variance(1)

            def angles():
                count = [0]

                def chain(done):
                    count[0] += 1
                    done.then_inc(table_step, 1)
                    dve.wait_ge(table_step, count[0])

                dve.wait_ge(pos_loaded, 32)
                chain(vec.tensor_copy(posf[:], posi[:]))
                for t in range(TT):
                    chain(vec.tensor_scalar(ang[:, t, :], invf[:], posf[:, t:t + 1], None, ALU.mult))
                chain(vec.tensor_scalar(kk[:], ang[:], 1.0 / (2.0 * np.pi), ROUND, ALU.mult, ALU.add))
                chain(vec.tensor_scalar(kk[:], kk[:], ROUND, None, ALU.subtract))
                chain(vec.tensor_scalar(kh[:], kk[:], 1.0 / SPLIT, ROUND, ALU.mult, ALU.add))
                chain(vec.tensor_scalar(kh[:], kh[:], ROUND, SPLIT, ALU.subtract, ALU.mult))
                chain(vec.tensor_tensor(kl[:], kk[:], kh[:], ALU.subtract))
                flat = "p a b -> p (a b)"
                last = ang[:].rearrange(flat)
                r = red[:].rearrange(flat)
                for piece in two_pi_parts():
                    for k in (kh, kl):
                        chain(vec.scalar_tensor_tensor(r, k[:].rearrange(flat), -piece, last, ALU.mult, ALU.add))
                        last = r
                w, c = wrap[:].rearrange(flat), cred[:].rearrange(flat)

                def turn(a, over, by):
                    chain(vec.tensor_scalar(w, a, over, by, ALU.is_gt if over > 0 else ALU.is_lt, ALU.mult))
                    chain(vec.tensor_tensor(a, a, w, ALU.add))

                pi = float(np.pi)
                turn(r, pi, -2 * pi)
                turn(r, -pi, 2 * pi)
                chain(vec.tensor_scalar(c, r, pi / 2, None, ALU.add))
                turn(c, pi, -2 * pi)
                for a in (r, c):
                    vec.tensor_scalar(a, a, 3.1415925, -3.1415925, ALU.min, ALU.max).then_inc(angles_ready, 1)

            for j in range(G_V * SPG, (G_QK + 1) * SPG + 3):
                split(j + LEAD)
                if j == G_V * SPG + 4:
                    angles()

            def head(h, r):
                if r == 2:
                    dve.wait_ge(scores_ready, h + 1)
                    dve.wait_ge(probs_ready, h + 0)
                    vec.tensor_tensor(masked[:], ps[:, 4, 0:3 * P], mask[:], ALU.add).then_inc(scores_masked, 1)
                    dve.wait_ge(scores_masked, h + 1)
                    vec.reduce_max(mx[:, 0:1], masked[:, 0:P], AX.X)
                    vec.reduce_max(mx[:, 1:2], masked[:, P:3 * P], AX.X).then_inc(max_ready, 1)
                    dve.wait_ge(max_ready, h + 1)
                    vec.tensor_scalar(negm, mx, -SCALE, None, ALU.mult).then_inc(negmax_ready, 1)
                if r == 4:
                    dve.wait_ge(probs_T, h + 1)
                    dve.wait_ge(pv_ready, h + 0)
                    vec.tensor_copy(probsT[:], ps[:, 5, 0:3 * P]).then_inc(probsT_ready, 1)
                if r == 5:
                    vec.reciprocal(rden, den).then_inc(den_step, 1)
                    dve.wait_ge(den_step, 3 * h + 1)
                    vec.tensor_tensor(rden2, rden, rden, ALU.mult).then_inc(den_step, 1)
                    dve.wait_ge(den_step, 3 * h + 2)
                    dve.wait_ge(o_squares, TT * h + TT)
                    vec.tensor_tensor(rden2, oss, rden2, ALU.mult).then_inc(den_step, 1)
                    dve.wait_ge(den_step, 3 * h + 3)
                    vec.tensor_scalar(ovar, rden2, 1.0 / HD, EPS, ALU.mult, ALU.add).then_inc(o_var, 1)
                if r == 6:
                    dve.wait_ge(o_rstd, h + 1)
                    vec.tensor_tensor(oscale, orstd, rden, ALU.mult).then_inc(o_scale, 1)
                    dve.wait_ge(o_scale, h + 1)
                    for t in range(TT):
                        done = vec.tensor_scalar(osc[:, t, :], ps[:, 5, t * HD:(t + 1) * HD], oscale[:, t:t + 1],
                                                 None, ALU.mult)
                    done.then_inc(o_scaled, 1)
                if r == 7:
                    dve.wait_ge(merged_hi, h + 1)
                    here = ds(h, 1)
                    vec.scalar_tensor_tensor(alo[:, here, :].rearrange("p a b -> p (a b)"), ps[:, 5, 2 * P:4 * P],
                                             gain(C_ATTN + h), ahi[:, here, :].rearrange("p a b -> p (a b)").bitcast(f32),
                                             ALU.mult, ALU.subtract).then_inc(merged_attn, 1)

            dve.wait_ge(consts_ready, 6)
            with dve.Fori(0, NH // 2) as i:
                for n in range(2):
                    for r in range(SPG):
                        split((G_QK + 1 + n) * SPG + 3 + r + LEAD, i * (2 * SPG))
                        head(i * 2 + n, r)

            def conv_taps(b):
                y = cy[:, b % 4, :]
                dve.wait_ge(conv_u, b + 1)
                vec.scalar_tensor_tensor(y, uT[:, b % 2, 1:1 + SEQ], gain(C_WC + CB + b), y,
                                         ALU.mult, ALU.add).then_inc(conv_tap, 1)
                dve.wait_ge(conv_tap, 2 * b + 1)
                vec.scalar_tensor_tensor(y, uT[:, b % 2, 0:SEQ], gain(C_WC + b), y, ALU.mult, ALU.add).then_inc(conv_tap, 1)
                dve.wait_ge(conv_tap, 2 * b + 2)
                vec.tensor_tensor(y, ps[:, CONV_BANKS[b % 4], SEQ:2 * SEQ], y, ALU.mult).then_inc(conv_y, 1)

            def conv_scale(b):
                y = cy[:, b % 4, :]
                dve.wait_ge(conv_root, b + 1)
                vec.reciprocal(csq[:, b % 4, :], csq[:, b % 4, :]).then_inc(conv_rec, 1)
                dve.wait_ge(conv_rec, b + 1)
                vec.scalar_tensor_tensor(y, y, gain(C_CONV + b), csq[:, b % 4, :], ALU.mult, ALU.mult).then_inc(conv_norm, 1)

            def conv_lo(b):
                dve.wait_ge(conv_hi, b + 1)
                vec.tensor_tensor(alo[:, NH + b, :], cy[:, b % 4, :], ahi[:, NH + b, :].bitcast(f32),
                                  ALU.subtract).then_inc(merged_conv, 1)

            dve.wait_ge(scores_ready, NH)
            vec.memset(uT[:, :, 0:2], 0.0).then_inc(pad_ready, 1)
            for j in range((G_X + 1) * SPG + 3, G_XQ * SPG + SPG):
                g, s = divmod(j, SPG)
                split(j + LEAD)
                if g == G_X + 1:
                    for b in {3: (0, 1), 4: (2, 3)}.get(s, ()):
                        conv_taps(b)
                    for b in {6: (0, 1), 7: (2, 3)}.get(s, ()):
                        conv_scale(b)
                    for b in {7: (0, 1)}.get(s, ()):
                        conv_lo(b)
                if g == G_OUT:
                    for b in {0: (2, 3)}.get(s, ()):
                        conv_lo(b)
                    for b in {2: (4, 5), 3: (6, 7)}.get(s, ()):
                        conv_taps(b)
                    for b in {5: (4, 5), 6: (6, 7)}.get(s, ()):
                        conv_scale(b)
                    for b in {5: (4, 5), 6: (6, 7)}.get(s, ()):
                        conv_lo(b)
                if g > G_OUT:
                    if s == 0:
                        add_group(g - 1, g * SPG)
                    if s in (1, 2):
                        u = 2 * (g - G_OUT - 1) + s - 1
                        unit(U_H2 + u, KS * u, C_XATTN, bhi, blo)
                if g == G_XQ and s == 4:
                    variance(2)
            split(J_XO + LEAD)
            dve.wait_ge(q2_T, 2)
            vec.tensor_copy(q2T[:, 2:4, :].rearrange("p a b -> p (a b)"), ps[:, 7, :]).then_inc(q2T_ready[1], 1)

            def x_max(h):
                dve.wait_ge(xs_ready, h + 1)
                vec.reduce_max(xmx[:, h, :], ps[:, 4 + h, :].rearrange("p (t m) -> p t m", t=TT), AX.X).then_inc(xmax, 1)
                dve.wait_ge(xmax, h + 1)
                vec.tensor_scalar(xnegm[:, h, :], xmx[:, h, :], -SCALE, None, ALU.mult).then_inc(xneg, 1)

            def x_normalise(h):
                dve.wait_ge(xexp, TT * (h + 1))
                vec.reciprocal(xrd[:, h, :], xden[:, h, :]).then_inc(xrec, 1)
                dve.wait_ge(xrec, h + 1)
                for t in range(TT):
                    vec.tensor_scalar(xp[:, h, t, :], xp[:, h, t, :], xrd[:, h, t:t + 1], None, ALU.mult).then_inc(xnorm, 1)

            x_max(0)
            x_max(1)
            x_normalise(0)
            x_max(2)
            x_normalise(1)
            x_max(3)
            x_normalise(2)
            x_normalise(3)
            for h in range(1, NXH, 2):
                dve.wait_ge(xp_T, h + 1)
                vec.tensor_copy(xpT[:, h].rearrange("p a b -> p (a b)"), ps[:, 4 + h, :]).then_inc(xpT_ready[1], 1)
            for h in range(NXH):
                dve.wait_ge(xo_hi, h + 1)
                vec.tensor_tensor(oxlo[:, h, :], ps[:, 4 + h, 0:SEQ], oxhi[:, h, :].bitcast(f32),
                                  ALU.subtract).then_inc(xo_lo, 1)
            dve.wait_ge(squares, 3 * TT)
            for j in range(J_XO + 1, J_FF):
                split(j + LEAD)
                n = j - J_XO
                if n % SXO == 0:
                    add_group(G_XO + n // SXO - 1, j)
                if n % SXO == 1 and n > SXO:
                    for m in range(2):
                        u = 2 * (n // SXO - 1) + m
                        unit(U_H3 + u, KS * u, C_FFN, ahi, alo)

            def up(c, ci=0):
                await_out(dve, G_FF + 2 * c, ci)
                dve.wait_ge(step_used, ci * (2 * SPG) + (J_FF + (2 * c + 2) * SPG))
                if not isinstance(ci, int) or c + ci > 0:
                    dve.wait_ge(unit_T, ci * 2 + (U_FF + 2 * c))
                for t in range(TT):
                    done = vec.scalar_tensor_tensor(fact[:, t, :], ps[:, 2 * ((G_FF + 1) % 2) + t, :], rstd[:, 3, t:t + 1],
                                                    silu[:, t, :], ALU.mult, ALU.mult)
                done.then_inc(evacuated[(G_FF + 1) % 2], 1)

            for s in range(2 * SPG):
                split(J_FF + s + LEAD)
                if s == 0:
                    add_group(G_FF - 1, J_FF)
                if s == 1:
                    for u in (SPG - 2, SPG - 1):
                        unit(U_H3 + u, KS * u, C_FFN, ahi, alo)
                if s == 3:
                    variance(3)
            with dve.Fori(0, NFC - 1) as ci:
                for s in range(2 * SPG):
                    split(J_FF + 2 * SPG + s + LEAD, ci * (2 * SPG))
                    if s == 0:
                        up(0, ci)
                    if s in (2, 3):
                        unit(U_FF + s - 2, KS * (s - 2), None, fhi, flo, ui=ci * 2, uk=ci * (2 * KS))
            up(NFC - 1)
            for n in range(2):
                unit(U_FF + 2 * (NFC - 1) + n, 2 * KS * (NFC - 1) + KS * n, None, fhi, flo)

            def finish_group(g):
                add_group(G_DN + g, J_DN + (g + 1) * SDN)
                await_out(dve, G_DN + g)
                cols = slice(g * GC, (g + 1) * GC)
                for t in range(TT):
                    vec.tensor_tensor(yout[:, t, cols], res[:, t, cols], gfin[:, cols], ALU.mult).then_inc(gained, 1)

            for g in range(D // GC):
                for s in range(SDN):
                    split(J_DN + g * SDN + s + LEAD)
                    if g == 1 and s == 0:
                        dve.wait_ge(gfin_loaded, 16)
                    if g and s == 0:
                        finish_group(g - 1)
            finish_group(D // GC - 1)
            dve.wait_ge(part_ready, TT * (D // GC))
            vec.reduce_sum(fss[:], part[:], AX.X).then_inc(fsum_ready, 1)
            dve.wait_ge(fsum_ready, 1)
            vec.tensor_scalar(fvar[:], fss[:], 1.0 / D, EPS, ALU.mult, ALU.add).then_inc(fvar_ready, 1)
            dve.wait_ge(frstd_ready, 1)
            dve.wait_ge(gained, TT * (D // GC))
            for h in range(2):
                half = slice(h * (D // 2), (h + 1) * (D // 2))
                vec.tensor_scalar(yout[:, 1, half], yout[:, 1, half], frstd[:, 1:2], None,
                                  ALU.mult).then_inc(final_ready[1], 1)


def tiles(w):
    k, n = w.shape
    return w.reshape(k // (KS * P), KS, P, n // GC, GC).transpose(3, 0, 2, 1, 4).reshape(-1, P, KS * GC)


def kernel(**inputs):
    import concourse.bacc as bacc
    from concourse.bass_utils import run_bass_kernel_spmd

    a = {k: np.asarray(v) for k, v in inputs.items()}
    w_in = a["w_in"][0]
    q, k, v, c, b, x = (w_in[:, i * AW:(i + 1) * AW] for i in range(6))
    qk = np.stack([q.reshape(D, NH, HD), k.reshape(D, NH, HD)], axis=2).reshape(D, 2 * AW)
    gate, up = (a[n][0].reshape(D, NFC, GC) for n in ("w_gate", "w_up"))
    gate_up = np.stack([gate, up], axis=2).reshape(D, 2 * FF)
    stream = np.concatenate([tiles(w) for w in (a["w_xkv"][0], v, qk, c, b, x, a["w_out"][0], a["w_xq"][0],
                                                a["w_xo"][0], gate_up, a["w_down"][0])])
    params = np.concatenate([a[n].reshape(-1, P) for n in ("g_mix", "g_xattn", "g_mem", "g_ffn", "g_attn_out",
                                                           "g_conv_out", "w_conv", "b_conv")])
    freq = (10000.0 ** (-np.arange(0, HD, 2, dtype=np.float64) / HD)).astype(np.float32)
    arrays = {
        "w_stream": stream,
        "x_in": a["x"][0],
        "mem_in": a["mem"][0],
        "params": params,
        "positions": np.ascontiguousarray(a["positions"].reshape(TT, P).T),
        "inv_freq": np.tile(freq, (P, 1)),
        "g_final": a["g_final"].reshape(1, D),
    }
    nc = bacc.Bacc("TRN2", target_bir_lowering=False, num_devices=1)
    args = [nc.dram_tensor(n, v.shape, mybir.dt.from_np(v.dtype), kind="ExternalInput").ap() for n, v in arrays.items()]
    out = nc.dram_tensor("y_out", (SEQ, D), mybir.dt.float32, kind="ExternalOutput").ap()
    build(nc, *args, out)
    r = run_bass_kernel_spmd(nc, [{n: np.ascontiguousarray(v) for n, v in arrays.items()}], core_ids=[0])
    return r.results[0]["y_out"].reshape(1, SEQ, D)
```

```python
from contextlib import ExitStack

import numpy as np
import concourse.bass as bass
from concourse import mybir

D = 2048
SEQ = 256
P = 128
TT = SEQ // P
NH = 8
HD = 128
AW = NH * HD
CW = D - AW
CB = CW // HD
NXH = 4
XW = NXH * HD
FF = -(-(8 * D) // (3 * 256)) * 256
EPS = 1e-6
SCALE = HD ** -0.5
GC = 512
KS = 2
KD = D // P
SPG = KD // KS
RING = 4
LEAD = 2

G_V = 0
G_QK = G_V + AW // GC
G_C = G_QK + 2 * AW // GC
G_X = G_C + 2 * CW // GC
G_KX = G_X + CW // GC
G_OUT = G_KX + XW // GC
G_XQ = G_OUT + D // GC
G_VX = G_XQ + XW // GC
G_XO = G_VX + XW // GC
G_FF = G_XO + D // GC
NFC = FF // GC
G_DN = G_FF + 2 * NFC
J_XO = G_XO * SPG
SXO = XW // (KS * P)
J_FF = J_XO + SXO * (D // GC)
J_DN = J_FF + 2 * NFC * SPG
SDN = FF // (KS * P)
STEPS = J_DN + SDN * (D // GC)

C_MIX, C_XATTN, C_MEM, C_FFN = 0, KD, 2 * KD, 3 * KD
C_ATTN = 4 * KD
C_CONV = C_ATTN + NH
C_WC = C_CONV + CB
C_BC = C_WC + 3 * CB
NPAR = C_BC + CB

U_H2, U_H3, U_FF = 0, SPG, 2 * SPG
CONV_START = {(G_X + 1) * SPG + 4 + 2 * b: b for b in range(CB)}
CONV_BANKS = (6, 7, 4, 5)
X_LOAD, X_SQUARES, FIRST_OUT = 3, (9, 11), 13
MEM_LOAD, MEM_SQUARES = 13, (20, 22)
ANGLES, TABLES = (8, 9, 10, 14, 15), 18
MASKED = -3.0e38
ROUND = 1.5 * 2.0 ** 23
SPLIT = 2.0 ** 11
WARM = 14


def two_pi_parts():
    parts, rest = [], 2.0 * np.pi
    for _ in range(4):
        unit = 2.0 ** (np.floor(np.log2(abs(rest))) - 11)
        parts.append(float(np.round(rest / unit) * unit))
        rest -= parts[-1]
    return parts


def build(nc, stream, x, xT, mem, memT, params, pos, inv_freq, g_final, out):
    f32, f32r, i32 = mybir.dt.float32, mybir.dt.float32r, mybir.dt.int32
    ALU, ACT, AX = mybir.AluOpType, mybir.ActivationFunctionType, mybir.AxisListType
    ds = bass.ds
    ctx = ExitStack()
    with ctx:
        top = nc.sbuf_base if isinstance(nc.sbuf_base, int) else nc.sbuf_base()
        place = [-(-top // 64) * 64]

        def sb(name, shape, dt=f32, at=None):
            size = 4 * int(np.prod(shape[1:]))
            where = place[0] if at is None else at[0]
            if at is None:
                place[0] += -(-size // 64) * 64
            else:
                at[0] += -(-size // 64) * 64
            return nc.alloc_sbuf_tensor_at(name, shape, dt, offset=where)

        def sem(name):
            return ctx.enter_context(nc.semaphore(name))

        res = sb("res", [P, TT, D])
        raw = sb("raw", [P, RING, KS * GC])
        whi = sb("whi", [P, RING, KS * GC], f32r)
        wlo = sb("wlo", [P, RING, KS * GC], f32r)
        yout = sb("yout", [P, TT, D], at=[place[0]])
        ahi = sb("ahi", [P, KD, SEQ], f32r)
        alo = sb("alo", [P, KD, SEQ], f32r)
        ident = sb("ident", [P, P])
        ones = sb("ones", [P, P])
        par = sb("par", [P, NPAR])
        mhalf = sb("mhalf", [P, TT])
        ssq = sb("ssq", [P, 4, TT])
        rstd = sb("rstd", [P, 4, TT])
        vpe = sb("vpe", [P, 4, TT])
        part = sb("part", [P, TT, D // GC])
        cvar = sb("cvar", [P, CB, TT])
        crstd = sb("crstd", [P, CB, TT])
        fss = sb("fss", [P, TT])
        fvar = sb("fvar", [P, TT])
        frstd = sb("frstd", [P, TT])
        shared = place[0]
        b_at = [place[0]]
        bhi = sb("bhi", [P, KD, SEQ], f32r)
        blo = sb("blo", [P, KD, SEQ], f32r)
        kxT = sb("kxT", [P, NXH, SEQ])
        proj_at = place[0]
        proj = sb("proj", [P, TT, G_KX * GC])
        mask = sb("mask", [P, 3 * P])
        cos = sb("cos", [P, TT, 2, HD // 2])
        sin = sb("sin", [P, TT, 2, HD // 2])
        probs = sb("probs", [P, 3 * P])
        probsT = sb("probsT", [P, 3 * P])
        masked = sb("masked", [P, 3 * P])
        osc = sb("osc", [P, TT, HD])
        small = sb("small", [P, 16, TT])
        mx, negm, den, rden, rden2, oss, ovar, orstd, oscale = (small[:, n, :] for n in range(9))
        conv_at = [place[0]]
        qkr = sb("qkr", [P, 2, TT, 2, HD])
        rtmp = sb("rtmp", [P, 4, TT, 2, HD // 2])
        qkT = sb("qkT", [P, 4, P])
        assert place[0] <= nc.sbuf_usable_end, (place[0], nc.sbuf_usable_end)
        uT = sb("uT", [P, 2, 2 + SEQ], at=conv_at)
        cy = sb("cy", [P, 4, SEQ], at=conv_at)
        csq = sb("csq", [P, 4, SEQ], at=conv_at)
        place[0] = max(place[0], conv_at[0])
        assert place[0] <= nc.sbuf_usable_end, (place[0], nc.sbuf_usable_end)
        par_cols = G_KX * GC
        late = 3 * AW
        stage = sb("stage", [P, KD, SEQ], at=[proj_at + 4 * (TT * par_cols - KD * SEQ)])
        memx = stage[:].rearrange("p k t -> p (k t)").rearrange("p (t d) -> p t d", t=TT)
        prep_at = [proj_at + 4 * late]
        posi = sb("posi", [P, TT], i32, at=prep_at)
        posf = sb("posf", [P, TT], at=prep_at)
        invf = sb("invf", [P, HD // 2], at=prep_at)
        ang, kk, kh, kl, red, cred, wrap = (sb(n, [P, TT, HD // 2], at=prep_at)
                                            for n in ("ang", "kk", "kh", "kl", "red", "cred", "wrap"))
        assert prep_at[0] <= proj_at + 4 * par_cols
        mT = [proj[:, h, 0:D].rearrange("p (k t) -> p k t", t=SEQ) for h in range(2)]
        kx = proj[:, :, D:D + XW]
        assert D + XW <= late
        xat = [proj_at + 4 * late]
        q2 = sb("q2", [P, TT, XW], at=xat)
        q2T = sb("q2T", [P, NXH, SEQ], at=xat)
        assert xat[0] <= proj_at + 4 * par_cols
        xat = [proj_at + 4 * (par_cols + late)]
        xsm = sb("xsm", [P, 4, NXH, TT], at=xat)
        xmx, xnegm, xden, xrd = (xsm[:, n] for n in range(4))
        junk1 = sb("junk1", [P, D], at=xat)
        assert xat[0] <= proj_at + 4 * 2 * par_cols
        vx = sb("vx", [P, TT, XW], at=b_at)
        xp = sb("xp", [P, NXH, TT, SEQ], at=b_at)
        xpT = sb("xpT", [P, NXH, TT, SEQ], at=b_at)
        oxhi = sb("oxhi", [P, NXH, SEQ], f32r, at=b_at)
        oxlo = sb("oxlo", [P, NXH, SEQ], f32r, at=b_at)
        assert b_at[0] <= proj_at
        fat = [shared]
        fhi = sb("fhi", [P, FF // P, SEQ], f32r, at=fat)
        flo = sb("flo", [P, FF // P, SEQ], f32r, at=fat)
        silu = sb("silu", [P, TT, GC], at=fat)
        fact = sb("fact", [P, TT, GC], at=fat)
        gfin = sb("gfin", [P, D], at=fat)
        junk2 = sb("junk2", [P, GC], at=fat)
        assert fat[0] <= nc.sbuf_usable_end, (fat[0], nc.sbuf_usable_end)
        ps = ctx.enter_context(nc.psum_tensor("ps", [P, 8, GC], f32))

        w_loaded = [sem(f"w_loaded{s}") for s in range(RING)]
        hi_ready = sem("hi_ready")
        lo_ready = sem("lo_ready")
        step_used = sem("step_used")
        evacuated = [sem("even_evacuated"), sem("odd_evacuated")]
        tile0_done = sem("tile0_done")
        xT_loaded = [sem(f"xT_loaded{u}") for u in range(SPG)]
        x_loaded = [sem("x0_loaded"), sem("x1_loaded")]
        mem_loaded, memT_loaded = [sem("mem0_loaded"), sem("mem1_loaded")], sem("memT_loaded")
        x_hi, x_lo, m_hi, m_lo = (sem(n) for n in ("x_hi", "x_lo", "m_hi", "m_lo"))
        vx_by_dve = sem("vx_by_dve")
        par_loaded, pos_loaded, gfin_loaded = sem("par_loaded"), sem("pos_loaded"), sem("gfin_loaded")
        blank, consts_ready = sem("blank"), sem("consts_ready")
        unit_T, unit_hi, unit_lo = sem("unit_T"), sem("unit_hi"), sem("unit_lo")
        squares, var_ready, rstd_ready = sem("squares"), sem("var_ready"), sem("rstd_ready")
        table_step, angles_ready, table_ready = sem("table_step"), sem("angles_ready"), sem("table_ready")
        kx_T, kxT_ready = sem("kx_T"), sem("kxT_ready")
        rope_products, rope_done = sem("rope_products"), sem("rope_done")
        qk_T, qkT_ready = sem("qk_T"), sem("qkT_ready")
        scores_ready, scores_masked = sem("scores_ready"), sem("scores_masked")
        max_ready, negmax_ready = sem("max_ready"), sem("negmax_ready")
        probs_ready, probs_T, probsT_ready = sem("probs_ready"), sem("probs_T"), sem("probsT_ready")
        pv_ready, o_squares, den_step = sem("pv_ready"), sem("o_squares"), sem("den_step")
        o_var, o_rstd, o_scale, o_scaled = sem("o_var"), sem("o_rstd"), sem("o_scale"), sem("o_scaled")
        o_T, merged_hi, merged_attn = sem("o_T"), sem("merged_hi"), sem("merged_attn")
        u_ready, conv_T, conv_u = sem("u_ready"), sem("conv_T"), sem("conv_u")
        conv_tap, conv_y, conv_sq = sem("conv_tap"), sem("conv_y"), sem("conv_sq")
        conv_ss, conv_var, conv_root = sem("conv_ss"), sem("conv_var"), sem("conv_root")
        conv_diag, conv_spread = sem("conv_diag"), sem("conv_spread")
        conv_norm, conv_hi, merged_conv = sem("conv_norm"), sem("conv_hi"), sem("merged_conv")
        pad_ready = sem("pad_ready")
        q2_T, q2T_ready = sem("q2_T"), [sem("q2T_by_act"), sem("q2T_by_dve")]
        xs_ready, xmax, xneg, xexp = sem("xs_ready"), sem("xmax"), sem("xneg"), sem("xexp")
        xrec, xnorm, xp_T = sem("xrec"), sem("xnorm"), sem("xp_T")
        xpT_ready = [sem("xpT_by_act"), sem("xpT_by_dve")]
        xo_ready, xo_hi, xo_lo = sem("xo_ready"), sem("xo_hi"), sem("xo_lo")
        part_ready, fsum_ready, fvar_ready, frstd_ready = (
            sem(n) for n in ("part_ready", "fsum_ready", "fvar_ready", "frstd_ready"))
        added = sem("added")
        gained = [sem("gained0"), sem("gained1")]
        final_ready, stored = [sem("final_by_act"), sem("final_by_dve")], sem("stored")

        block = ctx.enter_context(nc.Block())

        def conv_blocks(j, later):
            return [CONV_START[j - later]] if j - later in CONV_START else []

        def tile_pair(buf, j):
            return buf[:, j % RING, :]

        def loaded_by(j, it):
            return 16 * (j // RING + 1) + it * (16 // RING)

        def await_out(eng, g, gi=0):
            eng.wait_ge(evacuated[g % 2], gi + (g // 2 + 1))

        def gain(col):
            return par[:, ds(col, 1)]

        def unit_bank(u):
            return 6 + u % 2

        @block.sync
        def _(sp):
            for s in range(SPG):
                sp.dma_start(stage[:, KS * s:KS * (s + 1), :], xT[:, KS * s:KS * (s + 1), :]).then_inc(xT_loaded[s], 16)
                if s >= RING:
                    sp.wait_ge(lo_ready, s - RING + 1)
                sp.dma_start(tile_pair(raw, s), stream[s]).then_inc(w_loaded[s % RING], 16)
            with sp.Fori(SPG // RING, STEPS // RING) as i:
                for s in range(RING):
                    sp.wait_ge(lo_ready, i * RING + (s - RING + 1))
                    sp.dma_start(tile_pair(raw, s), stream[i * RING + s]).then_inc(w_loaded[s], 16)
            for t in range(TT):
                for h in range(2):
                    sp.wait_ge(final_ready[h], t + 1)
                    sp.dma_start(out[t * P:(t + 1) * P, h * (D // 2):(h + 1) * (D // 2)],
                                 yout[:, t, h * (D // 2):(h + 1) * (D // 2)]).then_inc(stored, 16)
            sp.wait_ge(stored, 16 * TT * 2)

        @block.gpsimd
        def _(pool):
            pool.memset(ident[:], 0.0).then_inc(blank, 1)
            pool.memset(mask[:], 0.0).then_inc(blank, 1)
            pool.memset(ones[:], 1.0).then_inc(consts_ready, 1)
            pool.memset(mhalf[:], -0.5).then_inc(consts_ready, 1)
            pool.wait_ge(blank, 2)
            pool.affine_select(out=ident[:], in_=ident[:], compare_op=ALU.not_equal, fill=1.0, base=0,
                               pattern=[[-1, P]], channel_multiplier=1).then_inc(consts_ready, 1)
            for n in (0, 2):
                pool.affine_select(out=mask[:, n * P:(n + 1) * P], in_=mask[:, n * P:(n + 1) * P],
                                   compare_op=ALU.is_ge, fill=MASKED, base=0,
                                   pattern=[[-1, P]], channel_multiplier=1).then_inc(consts_ready, 1)

            def root(n):
                pool.wait_ge(var_ready, n + 1)
                nc.gpsimd.tensor_tensor(rstd[:, n, :], vpe[:, n, :], mhalf[:], ALU.pow).then_inc(rstd_ready, 1)

            def rope(h, parity):
                src = proj[:, :, ds(AW + h * (2 * HD), 2 * HD)].rearrange("p t (q f) -> p t q f", q=2)
                lo_half, hi_half = src[:, :, :, 0:HD // 2], src[:, :, :, HD // 2:HD]
                pool.wait_ge(rope_done, 2 * h)
                for n, (a, b) in enumerate(((lo_half, cos), (hi_half, sin), (hi_half, cos), (lo_half, sin))):
                    nc.gpsimd.tensor_tensor(rtmp[:, n], a, b[:], ALU.mult).then_inc(rope_products, 1)
                pool.wait_ge(rope_products, 4 * h + 4)
                dst = qkr[:, parity]
                nc.gpsimd.tensor_tensor(dst[:, :, :, 0:HD // 2], rtmp[:, 0], rtmp[:, 1], ALU.subtract).then_inc(rope_done, 1)
                nc.gpsimd.tensor_tensor(dst[:, :, :, HD // 2:HD], rtmp[:, 2], rtmp[:, 3], ALU.add).then_inc(rope_done, 1)

            def head_root(h):
                pool.wait_ge(o_var, h + 1)
                nc.gpsimd.tensor_tensor(orstd, ovar, mhalf[:], ALU.pow).then_inc(o_rstd, 1)

            pool.wait_ge(consts_ready, 2)
            root(0)
            root(1)
            pool.wait_ge(table_ready, 4)
            await_out(pool, G_QK)
            rope(0, 0)
            rope(1, 1)
            with pool.Fori(0, NH // 2 - 1) as i:
                for n in range(2):
                    h = i * 2 + n
                    head_root(h)
                    pool.wait_ge(qk_T, h + 1)
                    rope(h + 2, n)
            head_root(NH - 2)
            head_root(NH - 1)
            c0, x0 = (G_C - G_V) * GC, (G_X - G_V) * GC
            for n in range(2):
                await_out(pool, G_X + n)
                u = proj[:, :, x0 + n * GC:x0 + (n + 1) * GC]
                nc.gpsimd.tensor_tensor(u, proj[:, :, c0 + n * GC:c0 + (n + 1) * GC], u, ALU.mult).then_inc(u_ready, 1)
                for j in range((G_X + 1) * SPG, G_KX * SPG + 1) if n == 0 else range(G_KX * SPG + 1, G_XQ * SPG):
                    for b in conv_blocks(j, 2):
                        pool.wait_ge(conv_var, b + 1)
                        nc.gpsimd.tensor_tensor(crstd[:, b, :], cvar[:, b, :], mhalf[:], ALU.pow).then_inc(conv_root, 1)
                    for b in conv_blocks(j, 5):
                        pool.wait_ge(conv_hi, b + 1)
                        nc.gpsimd.tensor_tensor(alo[:, NH + b, :], cy[:, b % 4, :], ahi[:, NH + b, :].bitcast(f32),
                                                ALU.subtract).then_inc(merged_conv, 1)
            root(2)
            root(3)
            for t in range(TT):
                pool.wait_ge(fvar_ready, t + 1)
                nc.gpsimd.tensor_tensor(frstd[:, t:t + 1], fvar[:, t:t + 1], mhalf[:, 0:1], ALU.pow).then_inc(frstd_ready, 1)

        @block.tensor
        def _(pe):
            def step(j, it, k, hi, lo, parity, first, last, token_tiles=range(TT)):
                pe.wait_ge(lo_ready, it + (j + 1))
                for t in token_tiles:
                    bank = ps[:, 2 * parity + t, :]
                    for n in range(KS):
                        w_h, w_l = (tile_pair(b, j)[:, n * GC:(n + 1) * GC] for b in (whi, wlo))
                        a_h, a_l = (b[:, k + n, t * P:(t + 1) * P] for b in (hi, lo))
                        nc.tensor.matmul(bank, lhsT=a_h, rhs=w_h, start=first and n == 0, stop=False)
                        nc.tensor.matmul(bank, lhsT=a_h, rhs=w_l, start=False, stop=False)
                        done = nc.tensor.matmul(bank, lhsT=a_l, rhs=w_h, start=False, stop=last and n == KS - 1)
                    if last and t == 0:
                        done.then_inc(tile0_done, 1)
                if TT - 1 in token_tiles:
                    done.then_inc(step_used, 1)

            def bank_free(g, gi=0):
                if g >= 2:
                    pe.wait_ge(evacuated[g % 2], gi + (g // 2))

            def group_step(g, s, hi, lo, it=0, gi=0, n_steps=SPG, j0=None):
                j = (g * SPG if j0 is None else j0) + s
                if s == 0:
                    bank_free(g, gi)
                step(j, it, KS * s, hi, lo, g % 2, s == 0, s == n_steps - 1)

            def unit(u, src, k):
                bank = ps[:, unit_bank(u), :].rearrange("p (k t) -> p k t", k=KS)
                for n in range(KS):
                    for t in range(TT):
                        done = nc.tensor.transpose(bank[:, n, t * P:(t + 1) * P],
                                                   src[:, t, (k + n) * P:(k + n + 1) * P], ident[:])
                done.then_inc(unit_T, 1)

            pe.wait_ge(consts_ready, 5)
            for _ in range(WARM):
                nc.tensor.matmul(ps[:, 7, 0:P], lhsT=ones[:], rhs=ones[:], start=True, stop=True)
            for g in range(G_V, G_QK + 2):
                for s in range(SPG if g <= G_QK else 3):
                    if g == G_V:
                        pe.wait_ge(x_lo, s + 1)
                    group_step(g, s, bhi, blo)

            def head_front(h, parity, stage):
                if stage == 0:
                    pe.wait_ge(rope_done, 2 * h + 2)
                    pe.wait_ge(scores_masked, h + 0)
                    for n in range(4):
                        done = nc.tensor.transpose(ps[:, 4, n * P:(n + 1) * P], qkr[:, parity, n % 2, n // 2, :], ident[:])
                    done.then_inc(qk_T, 1)
                if stage == 2:
                    pe.wait_ge(qkT_ready, h + 1)
                    nc.tensor.matmul(ps[:, 4, 0:P], lhsT=qkT[:, 0, :], rhs=qkT[:, 2, :], start=True, stop=True)
                    nc.tensor.matmul(ps[:, 4, P:3 * P], lhsT=qkT[:, 1, :], rhs=qkT[:, 2:4, :].rearrange("p a b -> p (a b)"),
                                     start=True, stop=True).then_inc(scores_ready, 1)
                if stage == 4:
                    pe.wait_ge(probs_ready, h + 1)
                    pe.wait_ge(merged_attn, h + 0)
                    for n in range(3):
                        done = nc.tensor.transpose(ps[:, 5, n * P:(n + 1) * P], probs[:, n * P:(n + 1) * P], ident[:])
                    done.then_inc(probs_T, 1)
                if stage == 5:
                    pe.wait_ge(probsT_ready, h + 1)
                    v0, v1 = (proj[:, t, ds(h * HD, HD)] for t in range(TT))
                    nc.tensor.matmul(ps[:, 5, 0:P], lhsT=probsT[:, 0:P], rhs=v0, start=True, stop=True)
                    nc.tensor.matmul(ps[:, 5, P:2 * P], lhsT=probsT[:, P:2 * P], rhs=v0, start=True, stop=False)
                    nc.tensor.matmul(ps[:, 5, P:2 * P], lhsT=probsT[:, 2 * P:3 * P], rhs=v1,
                                     start=False, stop=True).then_inc(pv_ready, 1)
                if stage == 7:
                    pe.wait_ge(o_scaled, h + 1)
                    for t in range(TT):
                        done = nc.tensor.transpose(ps[:, 5, (2 + t) * P:(3 + t) * P], osc[:, t, :], ident[:])
                    done.then_inc(o_T, 1)

            with pe.Fori(0, NH // 2) as i:
                for n in range(2):
                    for r in range(SPG):
                        head_front(i * 2 + n, n, r)
                        s = (3 + r) % SPG
                        g = G_QK + 1 + n + (3 + r) // SPG
                        group_step(g, s, bhi, blo, it=i * (2 * SPG), gi=i)

            def conv_front(b):
                pe.wait_ge(u_ready, b // 4 + 1)
                bank = CONV_BANKS[b % 4]
                if b == 3:
                    pe.wait_ge(merged_attn, NH)
                if b >= 4:
                    pe.wait_ge(conv_norm, b - 3)
                for n, c in enumerate(((G_X - G_V) * GC, (G_X - G_V) * GC - CW)):
                    for t in range(TT):
                        done = nc.tensor.transpose(ps[:, bank, (n * TT + t) * P:(n * TT + t + 1) * P],
                                                   proj[:, t, c + b * P:c + (b + 1) * P], ident[:])
                done.then_inc(conv_T, 1)

            def conv_sums(b):
                pe.wait_ge(conv_sq, b + 1)
                for t in range(TT):
                    done = nc.tensor.matmul(ps[:, CONV_BANKS[b % 4], SEQ + t:SEQ + t + 1],
                                            lhsT=csq[:, b % 4, t * P:(t + 1) * P], rhs=ones[:, 0:1], start=True, stop=True)
                done.then_inc(conv_ss, 1)

            def conv_spreading(b):
                pe.wait_ge(conv_diag, b + 1)
                nc.tensor.matmul(ps[:, CONV_BANKS[b % 4], 0:SEQ], lhsT=ones[:], rhs=csq[:, b % 4, :],
                                 start=True, stop=True).then_inc(conv_spread, 1)

            def conv_beside(j):
                for b in conv_blocks(j, 4):
                    conv_spreading(b)
                for b in conv_blocks(j, 2):
                    conv_sums(b)
                for b in conv_blocks(j, 0):
                    conv_front(b)

            for j in range((G_X + 1) * SPG + 3, G_OUT * SPG):
                g, s = divmod(j, SPG)
                conv_beside(j)
                if g == G_KX:
                    pe.wait_ge(m_lo, s + 1)
                group_step(g, s, bhi, blo)
            for g in range(G_OUT, G_XQ + 1):
                for s in range(SPG):
                    conv_beside(g * SPG + s)
                    if g == G_OUT:
                        if s == SPG - 1:
                            await_out(pe, G_KX)
                            pe.wait_ge(conv_norm, CB - 2)
                            for h in range(NXH):
                                for t in range(TT):
                                    at = ((h % 2) * TT + t) * P
                                    done = nc.tensor.transpose(ps[:, 6 + h // 2, at:at + P],
                                                               kx[:, t, h * HD:(h + 1) * HD], ident[:])
                            done.then_inc(kx_T, 1)
                        if s < NH // KS:
                            pe.wait_ge(merged_attn, KS * (s + 1))
                        else:
                            pe.wait_ge(merged_conv, KS * (s - NH // KS + 1))
                    elif s in (1, 2):
                        u = 2 * (g - G_OUT - 1) + s - 1
                        await_out(pe, g - 1)
                        if u == 0:
                            pe.wait_ge(kxT_ready, 1)
                        if u > 0:
                            pe.wait_ge(unit_lo, U_H2 + u - 1)
                        unit(U_H2 + u, res, KS * u)
                    if g == G_XQ:
                        pe.wait_ge(unit_lo, U_H2 + s + 1)
                        group_step(g, s, bhi, blo)
                    else:
                        group_step(g, s, ahi, alo)
            for s in range(SPG):
                if s == 1:
                    await_out(pe, G_XQ)
                    for h in range(NXH):
                        for t in range(TT):
                            at = ((h % 2) * TT + t) * P
                            done = nc.tensor.transpose(ps[:, 6 + h // 2, at:at + P], q2[:, t, h * HD:(h + 1) * HD], ident[:])
                        if h % 2:
                            done.then_inc(q2_T, 1)
                if s == 2:
                    for h in range(NXH):
                        if h % 2 == 0:
                            pe.wait_ge(q2T_ready[h // 2], 1)
                        if h == 2:
                            pe.wait_ge(q2T_ready[0], 1)
                        for t in range(TT):
                            done = nc.tensor.matmul(ps[:, 4 + h, t * SEQ:(t + 1) * SEQ], lhsT=q2T[:, h, t * P:(t + 1) * P],
                                                    rhs=kxT[:, h, :], start=True, stop=True)
                        done.then_inc(xs_ready, 1)
                if s == 6:
                    for h in range(NXH):
                        pe.wait_ge(xnorm, TT * (h + 1))
                        for m in range(TT):
                            for t in range(TT):
                                done = nc.tensor.transpose(ps[:, 4 + h, (m * TT + t) * P:(m * TT + t + 1) * P],
                                                           xp[:, h, t, m * P:(m + 1) * P], ident[:])
                        done.then_inc(xp_T, 1)
                pe.wait_ge(m_lo, SPG + s + 1)
                group_step(G_VX, s, ahi, alo)
            for m in range(TT):
                if m == 0:
                    await_out(pe, G_VX)
                else:
                    pe.wait_ge(vx_by_dve, 1)
                for h in range(NXH):
                    if m == 0:
                        pe.wait_ge(xpT_ready[h % 2], h // 2 + 1)
                    done = nc.tensor.matmul(ps[:, 4 + h, 0:SEQ], lhsT=vx[:, m, h * HD:(h + 1) * HD], rhs=xpT[:, h, m, :],
                                            start=m == 0, stop=m == TT - 1)
                    if m == TT - 1:
                        done.then_inc(xo_ready, 1)
            for g in range(G_XO, G_FF):
                for s in range(SXO):
                    if g > G_XO and s == 1:
                        await_out(pe, g - 1)
                        for u in (2 * (g - G_XO - 1), 2 * (g - G_XO - 1) + 1):
                            pe.wait_ge(unit_lo, U_H3 + u - 1)
                            unit(U_H3 + u, res, KS * u)
                    if g == G_XO:
                        pe.wait_ge(xo_lo, KS * (s + 1))
                    group_step(g, s, oxhi, oxlo, n_steps=SXO, j0=J_XO + SXO * (g - G_XO))

            def chunk(c, ci=0):
                for half in range(2):
                    for s in range(SPG):
                        if half == 0 and c == 0 and s == 1:
                            await_out(pe, G_FF - 1)
                            for u in (SPG - 2, SPG - 1):
                                pe.wait_ge(unit_lo, U_H3 + u - 1)
                                unit(U_H3 + u, res, KS * u)
                        if half == 0 and c == 0:
                            pe.wait_ge(unit_lo, U_H3 + s + 1)
                        if half == 0 and c == 1 and s in (2, 3):
                            ffn_unit(s - 2, ci)
                        group_step(G_FF + 2 * c + half, s, ahi, alo, it=ci * (2 * SPG), gi=ci,
                                   j0=J_FF + (2 * c + half) * SPG)

            def ffn_unit(n, ci):
                await_out(pe, G_FF + 1, ci)
                pe.wait_ge(unit_lo, ci * 2 + (U_FF + n - 1))
                unit(U_FF + n, fact, KS * n)

            chunk(0)
            with pe.Fori(0, NFC - 1) as ci:
                chunk(1, ci)
            ffn_unit(0, NFC - 1)
            ffn_unit(1, NFC - 1)
            with pe.Fori(0, D // GC // 2) as i:
                for n in range(2):
                    bank_free(G_DN + n, i)
                    pe.wait_ge(unit_lo, U_FF + 2 * (NFC - 1))

                    def down_step(s, token_tiles=range(TT)):
                        step(J_DN + n * SDN + s, i * (2 * SDN), KS * s, fhi, flo, (G_DN + n) % 2,
                             s == 0, s == SDN - 1, token_tiles)

                    for s in range(SDN - RING):
                        down_step(s)
                    pe.wait_ge(unit_lo, U_FF + 2 * NFC)
                    for t in range(TT):
                        for s in range(SDN - RING, SDN):
                            down_step(s, (t,))

        @block.scalar
        def _(act):
            act.dma_start(par[:], params).then_inc(par_loaded, 16)

            def cast(j, it=0):
                if isinstance(it, int) and j >= STEPS:
                    return
                act.wait_ge(w_loaded[j % RING], loaded_by(j, it))
                if j >= RING:
                    act.wait_ge(step_used, it + (j - RING + 1))
                nc.scalar.activation(tile_pair(whi, j), tile_pair(raw, j), ACT.Copy).then_inc(hi_ready, 1)

            def unit(u, k, col, hi, ui=0, uk=0):
                act.wait_ge(unit_T, ui + (u + 1))
                bank = ps[:, unit_bank(u), :].rearrange("p (k t) -> p k t", k=KS)
                if col is None:
                    done = nc.scalar.activation(hi[:, ds(uk + k, KS), :], bank, ACT.Copy)
                else:
                    for n in range(KS):
                        done = nc.scalar.activation(hi[:, k + n, :], bank[:, n, :], ACT.Copy, scale=gain(col + k + n))
                done.then_inc(unit_hi, 1)

            def token_squares(n, t, src, junk):
                if n or t:
                    act.wait_ge(squares, TT * n + t)
                nc.scalar.activation(junk, src[:, t, :], ACT.Square, accum_out=ssq[:, n, t:t + 1]).then_inc(squares, 1)

            def sum_squares(n, src, junk):
                for t in range(TT):
                    token_squares(n, t, src, junk)

            def evacuate(g, end, dst, scale, gi=0, steps=0, func=ACT.Copy):
                act.wait_ge(tile0_done, gi * 2 + (g + 1))
                for t in range(TT):
                    if t:
                        act.wait_ge(step_used, steps + end)
                    done = nc.scalar.activation(dst(t), ps[:, 2 * (g % 2) + t, :], func, scale=scale(t))
                done.then_inc(evacuated[g % 2], 1)

            def untransposed(k, src, col, hi, signal):
                for n in range(KS):
                    done = nc.scalar.activation(hi[:, k + n, :], src[:, n, :], ACT.Copy, scale=gain(col + k + n))
                done.then_inc(signal, 1)

            def mem_tiles(s):
                return mT[s // 4][:, KS * (s % 4):KS * (s % 4 + 1), :]

            def project(g, i=0):
                evacuate(g, SPG * (g + 1), lambda t: proj[:, t, ds(i * (2 * GC) + (g - G_V) * GC, GC)],
                         lambda t: rstd[:, 0, t:t + 1], gi=i, steps=i * (2 * SPG))

            side_banks = ps[:, 4:8, :].rearrange("p b n -> p (b n)")
            act.wait_ge(par_loaded, 16)
            for s in range(LEAD):
                act.wait_ge(xT_loaded[s], 16)
                untransposed(KS * s, stage[:, KS * s:KS * (s + 1), :], C_MIX, bhi, x_hi)
                cast(s)
            act.dma_start(posi[:], pos).then_inc(pos_loaded, 16)
            act.dma_start(invf[:], inv_freq).then_inc(pos_loaded, 16)
            for j in range((G_QK + 1) * SPG + 3):
                g, s = divmod(j, SPG)
                cast(j + LEAD)
                if j + LEAD < SPG:
                    k = KS * (j + LEAD)
                    act.wait_ge(xT_loaded[j + LEAD], 16)
                    untransposed(k, stage[:, k:k + KS, :], C_MIX, bhi, x_hi)
                for at, buf, src, loaded in ((X_LOAD, res, x, x_loaded), (MEM_LOAD, memx, mem, mem_loaded)):
                    if at <= j < at + 2 * TT:
                        t, h = divmod(j - at, 2)
                        if buf is memx and j == at:
                            act.wait_ge(x_lo, SPG)
                        act.dma_start(buf[:, t, h * (D // 2):(h + 1) * (D // 2)],
                                      src[t * P:(t + 1) * P, h * (D // 2):(h + 1) * (D // 2)]).then_inc(loaded[t], 16)
                if j in X_SQUARES:
                    t = X_SQUARES.index(j)
                    if t == 0:
                        act.wait_ge(step_used, 1)
                    act.wait_ge(x_loaded[t], 32)
                    token_squares(0, t, res, side_banks)
                if j in MEM_SQUARES:
                    t = MEM_SQUARES.index(j)
                    act.wait_ge(mem_loaded[t], 32)
                    token_squares(1, t, memx, side_banks)
                if j == FIRST_OUT:
                    act.wait_ge(rstd_ready, 1)
                    project(G_V)
                if s == 0 and g > G_V + 1:
                    project(g - 1)
                if j == TABLES:
                    act.wait_ge(angles_ready, 2)
                    for table, angle in ((sin, red), (cos, cred)):
                        for q in range(2):
                            nc.scalar.activation(table[:, :, q, :], angle[:], ACT.Sin).then_inc(table_ready, 1)

            def head(h, r):
                if r == 0:
                    act.wait_ge(qk_T, h + 1)
                    act.wait_ge(scores_ready, h + 0)
                    nc.scalar.activation(qkT[:].rearrange("p a b -> p (a b)"), ps[:, 4, :], ACT.Copy).then_inc(qkT_ready, 1)
                if r == 3:
                    act.wait_ge(negmax_ready, h + 1)
                    act.wait_ge(probs_T, h + 0)
                    nc.scalar.activation(probs[:, 0:P], masked[:, 0:P], ACT.Exp, bias=negm[:, 0:1], scale=SCALE,
                                         accum_out=den[:, 0:1])
                    nc.scalar.activation(probs[:, P:3 * P], masked[:, P:3 * P], ACT.Exp, bias=negm[:, 1:2], scale=SCALE,
                                         accum_out=den[:, 1:2]).then_inc(probs_ready, 1)
                if r == 5:
                    act.wait_ge(pv_ready, h + 1)
                    for t in range(TT):
                        if t:
                            act.wait_ge(o_squares, 2 * h + 1)
                        nc.scalar.activation(osc[:, 0, :], ps[:, 5, t * HD:(t + 1) * HD], ACT.Square,
                                             accum_out=oss[:, t:t + 1]).then_inc(o_squares, 1)
                if r == 7:
                    act.wait_ge(o_T, h + 1)
                    nc.scalar.activation(ahi[:, ds(h, 1), :].rearrange("p a b -> p (a b)"), ps[:, 5, 2 * P:4 * P],
                                         ACT.Copy, scale=gain(C_ATTN + h)).then_inc(merged_hi, 1)

            with act.Fori(0, NH // 2) as i:
                for n in range(2):
                    for r in range(SPG):
                        j = (G_QK + 1 + n) * SPG + 3 + r
                        cast(j + LEAD, i * (2 * SPG))
                        if r == 5:
                            project(G_QK + 1 + n, i)
                        head(i * 2 + n, r)

            def conv_in(b):
                act.wait_ge(conv_T, b + 1)
                if b == 0:
                    act.wait_ge(pad_ready, 1)
                if b >= 2:
                    act.wait_ge(conv_tap, 2 * (b - 1))
                if b >= 4:
                    act.wait_ge(merged_conv, b - 3)
                u = ps[:, CONV_BANKS[b % 4], 0:SEQ]
                nc.scalar.activation(uT[:, b % 2, 2:2 + SEQ], u, ACT.Copy)
                nc.scalar.activation(cy[:, b % 4, :], u, ACT.Identity, bias=gain(C_BC + b),
                                     scale=gain(C_WC + 2 * CB + b)).then_inc(conv_u, 1)

            def conv_square(b):
                act.wait_ge(conv_y, b + 1)
                if b >= 4:
                    act.wait_ge(conv_spread, b - 3)
                nc.scalar.activation(csq[:, b % 4, :], cy[:, b % 4, :], ACT.Square).then_inc(conv_sq, 1)

            def conv_out(b):
                act.wait_ge(conv_norm, b + 1)
                nc.scalar.activation(ahi[:, NH + b, :], cy[:, b % 4, :], ACT.Copy).then_inc(conv_hi, 1)

            act.wait_ge(pv_ready, NH)
            for h in range(2):
                act.dma_start(mT[h], memT[:, h * KD // 2:(h + 1) * KD // 2, :]).then_inc(memT_loaded, 16)
            for j in range((G_X + 1) * SPG + 3, J_XO):
                g, s = divmod(j, SPG)
                cast(j + LEAD)
                if g == G_KX and s == 0:
                    project(G_X + 1)
                if g == G_OUT and s == 0:
                    act.wait_ge(rstd_ready, 2)
                    evacuate(G_KX, j, lambda t: kx[:, t, :], lambda t: rstd[:, 1, t:t + 1])
                for b in conv_blocks(j, 0):
                    conv_in(b)
                for b in conv_blocks(j, 1):
                    conv_square(b)
                for b in conv_blocks(j, 5):
                    conv_out(b)
                u = j - (G_X + 1) * SPG - 6
                if 0 <= u < SPG:
                    if u == 0:
                        act.wait_ge(memT_loaded, 32)
                    act.wait_ge(step_used, (G_X + 1) * SPG + u + 1)
                    untransposed(KS * u, mem_tiles(u), C_MEM, bhi, m_hi)
                if g == G_XQ:
                    untransposed(KS * s, mem_tiles(s), C_MEM, ahi, m_hi)
                if g == G_OUT and s == SPG - 1:
                    act.wait_ge(kx_T, 1)
                    for n in range(NXH // 2):
                        done = nc.scalar.activation(kxT[:, 2 * n:2 * n + 2, :].rearrange("p a b -> p (a b)"),
                                                    ps[:, 6 + n, :], ACT.Copy)
                    done.then_inc(kxT_ready, 1)
                if G_OUT < g <= G_XQ and s in (1, 2):
                    u = 2 * (g - G_OUT - 1) + s - 1
                    unit(U_H2 + u, KS * u, C_XATTN, bhi)
                if g == G_XQ and s == 3:
                    await_out(act, G_XQ - 1)
                    sum_squares(2, res, junk1[:])
                if g == G_VX and s == 0:
                    act.wait_ge(rstd_ready, 3)
                    evacuate(G_XQ, j, lambda t: q2[:, t, :], lambda t: rstd[:, 2, t:t + 1])
                if g == G_VX and s == 1:
                    act.wait_ge(q2_T, 1)
                    nc.scalar.activation(q2T[:, 0:2, :].rearrange("p a b -> p (a b)"), ps[:, 6, :],
                                         ACT.Copy).then_inc(q2T_ready[0], 1)
                if g == G_VX and s in (2, 3):
                    for h in (2 * s - 4, 2 * s - 3):
                        act.wait_ge(xneg, h + 1)
                        for t in range(TT):
                            nc.scalar.activation(xp[:, h, t, :], ps[:, 4 + h, t * SEQ:(t + 1) * SEQ], ACT.Exp,
                                                 bias=xnegm[:, h, t:t + 1], scale=SCALE,
                                                 accum_out=xden[:, h, t:t + 1]).then_inc(xexp, 1)
                if g == G_VX and s == 6:
                    for h in range(0, NXH, 2):
                        act.wait_ge(xp_T, h + 1)
                        nc.scalar.activation(xpT[:, h].rearrange("p a b -> p (a b)"), ps[:, 4 + h, :],
                                             ACT.Copy).then_inc(xpT_ready[0], 1)
            cast(J_XO + LEAD)
            act.wait_ge(tile0_done, G_VX + 1)
            nc.scalar.activation(vx[:, 0, :], ps[:, 2 * (G_VX % 2), :], ACT.Copy,
                                 scale=rstd[:, 1, 0:1]).then_inc(evacuated[G_VX % 2], 1)
            for h in range(NXH):
                act.wait_ge(xo_ready, h + 1)
                nc.scalar.activation(oxhi[:, h, :], ps[:, 4 + h, 0:SEQ], ACT.Copy).then_inc(xo_hi, 1)
            for j in range(J_XO + 1, J_FF):
                cast(j + LEAD)
                if (j - J_XO) % SXO == 1 and j - J_XO > SXO:
                    for n in range(2):
                        u = 2 * ((j - J_XO) // SXO - 1) + n
                        unit(U_H3 + u, KS * u, C_FFN, ahi)

            def gate(c, ci=0):
                if isinstance(ci, int) and c == 0:
                    act.wait_ge(rstd_ready, 4)
                else:
                    await_out(act, G_FF + 2 * c - 1, ci)
                evacuate(G_FF + 2 * c, J_FF + (2 * c + 1) * SPG, lambda t: silu[:, t, :], lambda t: rstd[:, 3, t:t + 1],
                         gi=ci, steps=ci * (2 * SPG), func=ACT.Silu)

            for s in range(2 * SPG):
                j = J_FF + s
                cast(j + LEAD)
                if s == 1:
                    for u in (SPG - 2, SPG - 1):
                        unit(U_H3 + u, KS * u, C_FFN, ahi)
                if s == 2:
                    await_out(act, G_FF - 1)
                    sum_squares(3, res, junk1[:])
                if s == SPG:
                    gate(0)
            act.dma_start(gfin[:], g_final.partition_broadcast(P)).then_inc(gfin_loaded, 16)
            with act.Fori(0, NFC - 1) as ci:
                for s in range(2 * SPG):
                    cast(J_FF + 2 * SPG + s + LEAD, ci * (2 * SPG))
                    if s in (2, 3):
                        unit(U_FF + s - 2, KS * (s - 2), None, fhi, ui=ci * 2, uk=ci * (2 * KS))
                    if s == SPG:
                        gate(1, ci)
            for n in range(2):
                unit(U_FF + 2 * (NFC - 1) + n, 2 * KS * (NFC - 1) + KS * n, None, fhi)

            def result_squares(g, t):
                if t == 0:
                    act.wait_ge(added, g + 1)
                else:
                    await_out(act, G_DN + g)
                if g or t:
                    act.wait_ge(part_ready, TT * g + t)
                nc.scalar.activation(junk2[:], res[:, t, g * GC:(g + 1) * GC], ACT.Square,
                                     accum_out=part[:, t, g:g + 1]).then_inc(part_ready, 1)

            for g in range(D // GC):
                j = J_DN + g * SDN + LEAD
                for n in range(2):
                    cast(j + n)
                for t in range(TT if g else 0):
                    result_squares(g - 1, t)
                if g < D // GC - 1:
                    n_more = SDN - 2
                else:
                    n_more = SDN - 2 - LEAD
                with act.Fori(0, n_more // RING) as i:
                    for n in range(RING):
                        cast(j + 2 + n, i * RING)
                for n in range(n_more // RING * RING, n_more):
                    cast(j + 2 + n)
            for t in range(TT):
                result_squares(D // GC - 1, t)
                act.wait_ge(frstd_ready, t + 1)
                act.wait_ge(gained[t], D // GC)
                nc.scalar.activation(yout[:, t, 0:D // 2], yout[:, t, 0:D // 2], ACT.Copy,
                                     scale=frstd[:, t:t + 1]).then_inc(final_ready[0], 1)

        @block.vector
        def _(dve):
            vec = nc.vector

            def split(j, it=0):
                if isinstance(it, int) and j >= STEPS:
                    return
                dve.wait_ge(hi_ready, it + (j + 1))
                vec.tensor_tensor(tile_pair(wlo, j), tile_pair(raw, j), tile_pair(whi, j).bitcast(f32),
                                  ALU.subtract).then_inc(lo_ready, 1)

            def unit(u, k, col, hi, lo, ui=0, uk=0):
                dve.wait_ge(unit_hi, ui + (u + 1))
                bank = ps[:, unit_bank(u), :].rearrange("p (k t) -> p k t", k=KS)
                if col is None:
                    here = ds(uk + k, KS)
                    done = vec.tensor_tensor(lo[:, here, :], bank, hi[:, here, :].bitcast(f32), ALU.subtract)
                else:
                    for n in range(KS):
                        done = vec.scalar_tensor_tensor(lo[:, k + n, :], bank[:, n, :], gain(col + k + n),
                                                        hi[:, k + n, :].bitcast(f32), ALU.mult, ALU.subtract)
                done.then_inc(unit_lo, 1)

            def variance(n):
                dve.wait_ge(squares, TT * (n + 1))
                vec.tensor_scalar(vpe[:, n, :], ssq[:, n, :], 1.0 / D, EPS, ALU.mult, ALU.add).then_inc(var_ready, 1)

            def add_group(g, end):
                first = G_DN if g >= G_DN else G_XO if g >= G_XO else G_OUT
                dve.wait_ge(tile0_done, g + 1)
                for t in range(TT):
                    if t:
                        dve.wait_ge(step_used, end)
                    cols = res[:, t, (g - first) * GC:(g - first + 1) * GC]
                    done = vec.tensor_tensor(cols, ps[:, 2 * (g % 2) + t, :], cols, ALU.add)
                done.then_inc(evacuated[g % 2], 1)

            def untransposed(k, src, col, hi, lo, hi_signal, count, signal):
                dve.wait_ge(hi_signal, count)
                for n in range(KS):
                    done = vec.scalar_tensor_tensor(lo[:, k + n, :], src[:, n, :], gain(col + k + n),
                                                    hi[:, k + n, :].bitcast(f32), ALU.mult, ALU.subtract)
                done.then_inc(signal, 1)

            def mem_tiles(s):
                return mT[s // 4][:, KS * (s % 4):KS * (s % 4 + 1), :]

            chained = [0]

            def angles(piece):
                def chain(done):
                    chained[0] += 1
                    done.then_inc(table_step, 1)
                    dve.wait_ge(table_step, chained[0])

                flat = "p a b -> p (a b)"
                r, w, c = (a[:].rearrange(flat) for a in (red, wrap, cred))
                if piece == 0:
                    dve.wait_ge(pos_loaded, 32)
                    chain(vec.tensor_copy(posf[:], posi[:]))
                    for t in range(TT):
                        chain(vec.tensor_scalar(ang[:, t, :], invf[:], posf[:, t:t + 1], None, ALU.mult))
                    chain(vec.tensor_scalar(kk[:], ang[:], 1.0 / (2.0 * np.pi), ROUND, ALU.mult, ALU.add))
                    chain(vec.tensor_scalar(kk[:], kk[:], ROUND, None, ALU.subtract))
                if piece == 1:
                    chain(vec.tensor_scalar(kh[:], kk[:], 1.0 / SPLIT, ROUND, ALU.mult, ALU.add))
                    chain(vec.tensor_scalar(kh[:], kh[:], ROUND, SPLIT, ALU.subtract, ALU.mult))
                    chain(vec.tensor_tensor(kl[:], kk[:], kh[:], ALU.subtract))
                if piece in (1, 2):
                    for n, part_of_turn in enumerate(two_pi_parts()):
                        if n // 2 != piece - 1:
                            continue
                        for k in (kh, kl):
                            last = ang[:].rearrange(flat) if n == 0 and k is kh else r
                            chain(vec.scalar_tensor_tensor(r, k[:].rearrange(flat), -part_of_turn, last, ALU.mult, ALU.add))

                def turn(a, over, by):
                    chain(vec.tensor_scalar(w, a, over, by, ALU.is_gt if over > 0 else ALU.is_lt, ALU.mult))
                    chain(vec.tensor_tensor(a, a, w, ALU.add))

                pi = float(np.pi)
                if piece == 3:
                    turn(r, pi, -2 * pi)
                    turn(r, -pi, 2 * pi)
                if piece == 4:
                    chain(vec.tensor_scalar(c, r, pi / 2, None, ALU.add))
                    turn(c, pi, -2 * pi)
                    for a in (r, c):
                        vec.tensor_scalar(a, a, 3.1415925, -3.1415925, ALU.min, ALU.max).then_inc(angles_ready, 1)

            for s in range(LEAD):
                untransposed(KS * s, stage[:, KS * s:KS * (s + 1), :], C_MIX, bhi, blo, x_hi, s + 1, x_lo)
                split(s)
            for j in range((G_QK + 1) * SPG + 3):
                split(j + LEAD)
                if j + LEAD < SPG:
                    s = j + LEAD
                    untransposed(KS * s, stage[:, KS * s:KS * (s + 1), :], C_MIX, bhi, blo, x_hi, s + 1, x_lo)
                if j in ANGLES:
                    angles(ANGLES.index(j))
                if j == FIRST_OUT - 1:
                    variance(0)
                if j == MEM_SQUARES[-1]:
                    variance(1)

            def head(h, r):
                if r == 2:
                    dve.wait_ge(scores_ready, h + 1)
                    dve.wait_ge(probs_ready, h + 0)
                    vec.tensor_tensor(masked[:], ps[:, 4, 0:3 * P], mask[:], ALU.add).then_inc(scores_masked, 1)
                    dve.wait_ge(scores_masked, h + 1)
                    vec.reduce_max(mx[:, 0:1], masked[:, 0:P], AX.X)
                    vec.reduce_max(mx[:, 1:2], masked[:, P:3 * P], AX.X).then_inc(max_ready, 1)
                    dve.wait_ge(max_ready, h + 1)
                    vec.tensor_scalar(negm, mx, -SCALE, None, ALU.mult).then_inc(negmax_ready, 1)
                if r == 4:
                    dve.wait_ge(probs_T, h + 1)
                    dve.wait_ge(pv_ready, h + 0)
                    vec.tensor_copy(probsT[:], ps[:, 5, 0:3 * P]).then_inc(probsT_ready, 1)
                if r == 5:
                    vec.reciprocal(rden, den).then_inc(den_step, 1)
                    dve.wait_ge(den_step, 3 * h + 1)
                    vec.tensor_tensor(rden2, rden, rden, ALU.mult).then_inc(den_step, 1)
                    dve.wait_ge(den_step, 3 * h + 2)
                    dve.wait_ge(o_squares, TT * h + TT)
                    vec.tensor_tensor(rden2, oss, rden2, ALU.mult).then_inc(den_step, 1)
                    dve.wait_ge(den_step, 3 * h + 3)
                    vec.tensor_scalar(ovar, rden2, 1.0 / HD, EPS, ALU.mult, ALU.add).then_inc(o_var, 1)
                if r == 6:
                    dve.wait_ge(o_rstd, h + 1)
                    vec.tensor_tensor(oscale, orstd, rden, ALU.mult).then_inc(o_scale, 1)
                    dve.wait_ge(o_scale, h + 1)
                    for t in range(TT):
                        done = vec.tensor_scalar(osc[:, t, :], ps[:, 5, t * HD:(t + 1) * HD], oscale[:, t:t + 1],
                                                 None, ALU.mult)
                    done.then_inc(o_scaled, 1)
                if r == 7:
                    dve.wait_ge(merged_hi, h + 1)
                    here = ds(h, 1)
                    vec.scalar_tensor_tensor(alo[:, here, :].rearrange("p a b -> p (a b)"), ps[:, 5, 2 * P:4 * P],
                                             gain(C_ATTN + h), ahi[:, here, :].rearrange("p a b -> p (a b)").bitcast(f32),
                                             ALU.mult, ALU.subtract).then_inc(merged_attn, 1)

            dve.wait_ge(consts_ready, 5)
            with dve.Fori(0, NH // 2) as i:
                for n in range(2):
                    for r in range(SPG):
                        split((G_QK + 1 + n) * SPG + 3 + r + LEAD, i * (2 * SPG))
                        head(i * 2 + n, r)

            def conv_taps(b):
                y = cy[:, b % 4, :]
                dve.wait_ge(conv_u, b + 1)
                vec.scalar_tensor_tensor(y, uT[:, b % 2, 1:1 + SEQ], gain(C_WC + CB + b), y,
                                         ALU.mult, ALU.add).then_inc(conv_tap, 1)
                dve.wait_ge(conv_tap, 2 * b + 1)
                vec.scalar_tensor_tensor(y, uT[:, b % 2, 0:SEQ], gain(C_WC + b), y, ALU.mult, ALU.add).then_inc(conv_tap, 1)
                dve.wait_ge(conv_tap, 2 * b + 2)
                vec.tensor_tensor(y, ps[:, CONV_BANKS[b % 4], SEQ:2 * SEQ], y, ALU.mult).then_inc(conv_y, 1)

            def conv_mean(b):
                dve.wait_ge(conv_ss, b + 1)
                vec.tensor_scalar(cvar[:, b, :], ps[:, CONV_BANKS[b % 4], SEQ:SEQ + TT], 1.0 / HD, EPS,
                                  ALU.mult, ALU.add).then_inc(conv_var, 1)

            def conv_diagonal(b):
                dve.wait_ge(conv_root, b + 1)
                for t in range(TT):
                    done = vec.tensor_scalar(csq[:, b % 4, t * P:(t + 1) * P], ident[:], crstd[:, b, t:t + 1], None, ALU.mult)
                done.then_inc(conv_diag, 1)

            def conv_scale(b):
                y = cy[:, b % 4, :]
                dve.wait_ge(conv_spread, b + 1)
                vec.scalar_tensor_tensor(y, y, gain(C_CONV + b), ps[:, CONV_BANKS[b % 4], 0:SEQ],
                                         ALU.mult, ALU.mult).then_inc(conv_norm, 1)

            dve.wait_ge(scores_ready, NH)
            vec.memset(uT[:, :, 0:2], 0.0).then_inc(pad_ready, 1)

            def x_max(h):
                dve.wait_ge(xs_ready, h + 1)
                vec.reduce_max(xmx[:, h, :], ps[:, 4 + h, :].rearrange("p (t m) -> p t m", t=TT), AX.X).then_inc(xmax, 1)
                dve.wait_ge(xmax, h + 1)
                vec.tensor_scalar(xnegm[:, h, :], xmx[:, h, :], -SCALE, None, ALU.mult).then_inc(xneg, 1)

            def x_normalise(h):
                dve.wait_ge(xexp, TT * (h + 1))
                vec.reciprocal(xrd[:, h, :], xden[:, h, :]).then_inc(xrec, 1)
                dve.wait_ge(xrec, h + 1)
                for t in range(TT):
                    vec.tensor_scalar(xp[:, h, t, :], xp[:, h, t, :], xrd[:, h, t:t + 1], None, ALU.mult).then_inc(xnorm, 1)

            for j in range((G_X + 1) * SPG + 3, J_XO):
                g, s = divmod(j, SPG)
                split(j + LEAD)
                if G_OUT < g <= G_XQ and s == 0:
                    add_group(g - 1, g * SPG)
                for b in conv_blocks(j, 0):
                    conv_taps(b)
                for b in conv_blocks(j, 2):
                    conv_mean(b)
                for b in conv_blocks(j, 3):
                    conv_diagonal(b)
                for b in conv_blocks(j, 4):
                    conv_scale(b)
                u = j - (G_X + 1) * SPG - 6
                if 0 <= u < SPG:
                    untransposed(KS * u, mem_tiles(u), C_MEM, bhi, blo, m_hi, u + 1, m_lo)
                if g == G_XQ:
                    untransposed(KS * s, mem_tiles(s), C_MEM, ahi, alo, m_hi, SPG + s + 1, m_lo)
                if G_OUT < g <= G_XQ and s in (1, 2):
                    u = 2 * (g - G_OUT - 1) + s - 1
                    unit(U_H2 + u, KS * u, C_XATTN, bhi, blo)
                if g == G_XQ and s == 4:
                    variance(2)
                if g == G_VX and s == 1:
                    dve.wait_ge(q2_T, 2)
                    vec.tensor_copy(q2T[:, 2:4, :].rearrange("p a b -> p (a b)"), ps[:, 7, :]).then_inc(q2T_ready[1], 1)
                if g == G_VX and s == 2:
                    x_max(0)
                    x_max(1)
                    x_normalise(0)
                if g == G_VX and s == 3:
                    x_max(2)
                    x_normalise(1)
                    x_max(3)
                if g == G_VX and s == 4:
                    x_normalise(2)
                    x_normalise(3)
                if g == G_VX and s == 6:
                    for h in range(1, NXH, 2):
                        dve.wait_ge(xp_T, h + 1)
                        vec.tensor_copy(xpT[:, h].rearrange("p a b -> p (a b)"), ps[:, 4 + h, :]).then_inc(xpT_ready[1], 1)
            split(J_XO + LEAD)
            dve.wait_ge(step_used, J_XO)
            vec.tensor_scalar(vx[:, 1, :], ps[:, 2 * (G_VX % 2) + 1, :], rstd[:, 1, 1:2], None, ALU.mult).then_inc(vx_by_dve, 1)
            for h in range(NXH):
                dve.wait_ge(xo_hi, h + 1)
                vec.tensor_tensor(oxlo[:, h, :], ps[:, 4 + h, 0:SEQ], oxhi[:, h, :].bitcast(f32),
                                  ALU.subtract).then_inc(xo_lo, 1)
            dve.wait_ge(squares, 3 * TT)
            for j in range(J_XO + 1, J_FF):
                split(j + LEAD)
                n = j - J_XO
                if n % SXO == 0:
                    add_group(G_XO + n // SXO - 1, j)
                if n % SXO == 1 and n > SXO:
                    for m in range(2):
                        u = 2 * (n // SXO - 1) + m
                        unit(U_H3 + u, KS * u, C_FFN, ahi, alo)

            def up(c, ci=0):
                await_out(dve, G_FF + 2 * c, ci)
                dve.wait_ge(tile0_done, ci * 2 + (G_FF + 2 * c + 2))
                if not isinstance(ci, int) or c + ci > 0:
                    dve.wait_ge(unit_T, ci * 2 + (U_FF + 2 * c))
                for t in range(TT):
                    if t:
                        dve.wait_ge(step_used, ci * (2 * SPG) + (J_FF + (2 * c + 2) * SPG))
                    done = vec.scalar_tensor_tensor(fact[:, t, :], ps[:, 2 * ((G_FF + 1) % 2) + t, :], rstd[:, 3, t:t + 1],
                                                    silu[:, t, :], ALU.mult, ALU.mult)
                done.then_inc(evacuated[(G_FF + 1) % 2], 1)

            for s in range(2 * SPG):
                split(J_FF + s + LEAD)
                if s == 0:
                    add_group(G_FF - 1, J_FF)
                if s == 1:
                    for u in (SPG - 2, SPG - 1):
                        unit(U_H3 + u, KS * u, C_FFN, ahi, alo)
                if s == 3:
                    variance(3)
            with dve.Fori(0, NFC - 1) as ci:
                for s in range(2 * SPG):
                    split(J_FF + 2 * SPG + s + LEAD, ci * (2 * SPG))
                    if s == 0:
                        up(0, ci)
                    if s in (2, 3):
                        unit(U_FF + s - 2, KS * (s - 2), None, fhi, flo, ui=ci * 2, uk=ci * (2 * KS))
            up(NFC - 1)
            for n in range(2):
                unit(U_FF + 2 * (NFC - 1) + n, 2 * KS * (NFC - 1) + KS * n, None, fhi, flo)

            def finish_group(g, t):
                if t == 0:
                    dve.wait_ge(tile0_done, G_DN + g + 1)
                else:
                    dve.wait_ge(step_used, J_DN + (g + 1) * SDN)
                cols = slice(g * GC, (g + 1) * GC)
                done = vec.tensor_tensor(res[:, t, cols], ps[:, 2 * ((G_DN + g) % 2) + t, :], res[:, t, cols], ALU.add)
                if t == 0:
                    done.then_inc(added, 1)
                    dve.wait_ge(added, g + 1)
                else:
                    done.then_inc(evacuated[(G_DN + g) % 2], 1)
                    await_out(dve, G_DN + g)
                vec.tensor_tensor(yout[:, t, cols], res[:, t, cols], gfin[:, cols], ALU.mult).then_inc(gained[t], 1)

            for g in range(D // GC):
                j = J_DN + g * SDN + LEAD
                split(j)
                if g == 1:
                    dve.wait_ge(gfin_loaded, 16)
                for t in range(TT if g else 0):
                    finish_group(g - 1, t)
                n_more = SDN - 1 if g < D // GC - 1 else SDN - 1 - LEAD
                with dve.Fori(0, n_more // RING) as i:
                    for n in range(RING):
                        split(j + 1 + n, i * RING)
                for n in range(n_more // RING * RING, n_more):
                    split(j + 1 + n)
            for t in range(TT):
                finish_group(D // GC - 1, t)
                dve.wait_ge(part_ready, TT * (D // GC - 1) + t + 1)
                vec.reduce_sum(fss[:, t:t + 1], part[:, t, :], AX.X).then_inc(fsum_ready, 1)
                dve.wait_ge(fsum_ready, t + 1)
                vec.tensor_scalar(fvar[:, t:t + 1], fss[:, t:t + 1], 1.0 / D, EPS, ALU.mult, ALU.add).then_inc(fvar_ready, 1)
                dve.wait_ge(frstd_ready, t + 1)
                dve.wait_ge(gained[t], D // GC)
                vec.tensor_scalar(yout[:, t, D // 2:D], yout[:, t, D // 2:D], frstd[:, t:t + 1], None,
                                  ALU.mult).then_inc(final_ready[1], 1)


def tiles(w):
    k, n = w.shape
    return w.reshape(k // (KS * P), KS, P, n // GC, GC).transpose(3, 0, 2, 1, 4).reshape(-1, P, KS * GC)


def kernel(**inputs):
    import concourse.bacc as bacc
    from concourse.bass_utils import run_bass_kernel_spmd

    a = {k: np.asarray(v) for k, v in inputs.items()}
    w_in = a["w_in"][0]
    q, k, v, c, b, x = (w_in[:, i * AW:(i + 1) * AW] for i in range(6))
    qk = np.stack([q.reshape(D, NH, HD), k.reshape(D, NH, HD)], axis=2).reshape(D, 2 * AW)
    w_kx, w_vx = a["w_xkv"][0][:, :XW], a["w_xkv"][0][:, XW:]
    gate, up = (a[n][0].reshape(D, NFC, GC) for n in ("w_gate", "w_up"))
    gate_up = np.stack([gate, up], axis=2).reshape(D, 2 * FF)
    stream = np.concatenate([tiles(w) for w in (v, qk, c, b, x, w_kx, a["w_out"][0], a["w_xq"][0], w_vx,
                                                a["w_xo"][0], gate_up, a["w_down"][0])])
    params = np.concatenate([a[n].reshape(-1, P) for n in ("g_mix", "g_xattn", "g_mem", "g_ffn", "g_attn_out",
                                                           "g_conv_out", "w_conv", "b_conv")])
    freq = (10000.0 ** (-np.arange(0, HD, 2, dtype=np.float64) / HD)).astype(np.float32)
    arrays = {
        "w_stream": stream,
        "x_in": a["x"][0],
        "x_T": a["x"][0].T.reshape(KD, P, SEQ).transpose(1, 0, 2),
        "mem_in": a["mem"][0],
        "mem_T": a["mem"][0].T.reshape(KD, P, SEQ).transpose(1, 0, 2),
        "params": params.T,
        "positions": np.ascontiguousarray(a["positions"].reshape(TT, P).T),
        "inv_freq": np.tile(freq, (P, 1)),
        "g_final": a["g_final"].reshape(1, D),
    }
    nc = bacc.Bacc("TRN2", target_bir_lowering=False, num_devices=1)
    args = [nc.dram_tensor(n, v.shape, mybir.dt.from_np(v.dtype), kind="ExternalInput").ap() for n, v in arrays.items()]
    out = nc.dram_tensor("y_out", (SEQ, D), mybir.dt.float32, kind="ExternalOutput").ap()
    build(nc, *args, out)
    r = run_bass_kernel_spmd(nc, [{n: np.ascontiguousarray(v) for n, v in arrays.items()}], core_ids=[0])
    return r.results[0]["y_out"].reshape(1, SEQ, D)
```
